# Optimizing a Trainium2 kernel written in Bass

```python
import jax, jax.numpy as jnp
from jax import lax
import numpy as np

D_MODEL = 1024
BATCH = 1
SEQ = 128
DEPTH = 2
DEC_BATCH = 1
DEC_SEQ = 512
PAST_LEN = 128

GRID_W = 64
H_A = 4
DH_A = 96
D_A = H_A * DH_A
MLSTM_CHUNK = 64
H_B = 6
KV_B = 2
G_B = H_B // KV_B
HD_B = 64
D_B = H_B * HD_B
D_KVB = KV_B * HD_B
WIN = 128
WBLK = 128
ROPE_BASE = 10000.0
H_C = 4
HD_C = 64
D_C = H_C * HD_C
NA_WIN_H = 8
NA_WIN_W = 16
NA_QCOL = 16
NA_KCOL = NA_QCOL + NA_WIN_W
SPLIT_SIZES = (D_A, D_A, D_A, D_A, 2 * H_A, 2 * H_A, D_B, D_KVB, D_KVB, D_C, D_C, D_C)
D_IN = 4 * D_A + 4 * H_A + D_B + 2 * D_KVB + 3 * D_C
D_MIX = D_A + D_B + D_C
QBLK = 128
N_GROUPS = 4
E_PER_GROUP = 8
N_EXPERTS = N_GROUPS * E_PER_GROUP
TOP_K = 2
D_EXPERT = D_MODEL // 4
MOE_BLK = 128
ALPHA = (2 * DEPTH) ** 0.25
BETA = (8 * DEPTH) ** -0.25
LN_EPS = 1e-5

kernel_name = 'hybrid_mlstm_swa_natten_hmoe_diffusion_step'

def layer_norm(x, g, b):
    xf = x.astype(jnp.float32)
    mu = jnp.mean(xf, -1, keepdims=True)
    var = jnp.mean(jnp.square(xf - mu), -1, keepdims=True)
    y = (xf - mu) * lax.rsqrt(var + LN_EPS) * g.astype(jnp.float32) + b.astype(jnp.float32)
    return y.astype(x.dtype)

def adaln(cvec, w, b):
    mod = (jax.nn.silu(cvec) @ w + b)[:, None, :]
    return jnp.split(mod, 6, axis=-1)

def post_norm(x, y, gate, g, b):
    return layer_norm(ALPHA * x + gate * y, g, b)

def split_proj(z):
    pts, acc = [], 0
    for s in SPLIT_SIZES[:-1]:
        acc += s
        pts.append(acc)
    return jnp.split(z, pts, axis=-1)

def axial_rope(n_tok, hd):
    t = jnp.arange(n_tok)
    nf = hd // 4
    inv = ROPE_BASE ** (-jnp.arange(nf, dtype=jnp.float32) / nf)
    ar = (t // GRID_W).astype(jnp.float32)[:, None] * inv
    ac = (t % GRID_W).astype(jnp.float32)[:, None] * inv
    ang = jnp.concatenate([ar, ar, ac, ac], -1)
    return jnp.cos(ang), jnp.sin(ang)

def apply_rope(x, cos, sin):
    x1, x2, x3, x4 = jnp.split(x, 4, axis=-1)
    rot = jnp.concatenate([-x2, x1, -x4, x3], -1)
    return x * cos[:, None].astype(x.dtype) + rot * sin[:, None].astype(x.dtype)

def mlstm_chunkwise(q, k, v, ig, lf, C0, n0, m0):
    B, H, L, d = q.shape
    lc = min(MLSTM_CHUNK, L)
    nc = L // lc

    def to_chunks(a):
        return jnp.moveaxis(a.reshape(a.shape[:2] + (nc, lc) + a.shape[3:]), 2, 0)

    xs = tuple(to_chunks(a) for a in (q, k, v, ig, lf))
    causal = jnp.tril(jnp.ones((lc, lc), bool))

    def step(carry, inp):
        C, n, m = carry
        qc, kc, vc, ic, fc = inp
        b = jnp.cumsum(fc, -1)
        dmat = jnp.where(causal, b[..., :, None] - b[..., None, :] + ic[..., None, :], -jnp.inf)
        inter = b + m[..., None]
        m_out = jnp.maximum(inter, jnp.max(dmat, -1))
        wmat = jnp.exp(dmat - m_out[..., None])
        sw = jnp.einsum('bhtd,bhsd->bhts', qc, kc) * wmat
        sc_in = jnp.exp(inter - m_out)
        num = jnp.einsum('bhts,bhsd->bhtd', sw, vc) + sc_in[..., None] * jnp.einsum('bhvk,bhtk->bhtv', C, qc)
        den = jnp.sum(sw, -1) + sc_in * jnp.einsum('bhk,bhtk->bht', n, qc)
        h = num / jnp.maximum(jnp.abs(den), jnp.exp(-m_out))[..., None]
        bl = b[..., -1]
        dec = bl[..., None] - b + ic
        m_new = jnp.maximum(bl + m, jnp.max(dec, -1))
        wk = jnp.exp(dec - m_new[..., None])
        sc_st = jnp.exp(bl + m - m_new)
        C_new = sc_st[..., None, None] * C + jnp.einsum('bhs,bhsv,bhsk->bhvk', wk, vc, kc)
        n_new = sc_st[..., None] * n + jnp.einsum('bhs,bhsk->bhk', wk, kc)
        return (C_new, n_new, m_new), h

    (C, n, m), hs = lax.scan(step, (C0, n0, m0), xs)
    h = jnp.moveaxis(hs, 0, 2).reshape(B, H, L, d)
    return h, C, n, m

def mlstm_mixer(q, k, v, o_pre, i_pre, f_pre, b_i, b_f, w_norm, C0, n0, m0):
    B, L, _ = q.shape

    def heads(a):
        return jnp.moveaxis(a.reshape(B, L, H_A, DH_A), 1, 2).astype(jnp.float32)

    qh, kh, vh = heads(q), heads(k) * DH_A ** -0.5, heads(v)
    ig = jnp.moveaxis(i_pre.reshape(B, L, 2, H_A).astype(jnp.float32) + b_i.astype(jnp.float32), 1, -1)
    lf = jnp.moveaxis(jax.nn.log_sigmoid(f_pre.reshape(B, L, 2, H_A).astype(jnp.float32) + b_f.astype(jnp.float32)), 1, -1)
    C0, n0, m0 = C0.astype(jnp.float32), n0.astype(jnp.float32), m0.astype(jnp.float32)
    h_f, Cf, nf, mf = mlstm_chunkwise(qh, kh, vh, ig[:, 0], lf[:, 0], C0[:, 0], n0[:, 0], m0[:, 0])
    flip = lambda a: jnp.flip(a, axis=2)
    h_b, Cb, nb, mb = mlstm_chunkwise(flip(qh), flip(kh), flip(vh), flip(ig[:, 1]), flip(lf[:, 1]), C0[:, 1], n0[:, 1], m0[:, 1])
    h = jnp.moveaxis(h_f + flip(h_b), 1, 2)
    mu = jnp.mean(h, -1, keepdims=True)
    var = jnp.mean(jnp.square(h - mu), -1, keepdims=True)
    h = ((h - mu) * lax.rsqrt(var + LN_EPS)).reshape(B, L, D_A) * w_norm.astype(jnp.float32)
    out = (jax.nn.sigmoid(o_pre.astype(jnp.float32)) * h).astype(q.dtype)
    return out, jnp.stack([Cf, Cb], 1), jnp.stack([nf, nb], 1), jnp.stack([mf, mb], 1)

def ctx_attention(q, k, v, sink):
    B, L, KV, G, d = q.shape
    nq = L // QBLK
    qb = jnp.moveaxis(q.reshape(B, nq, QBLK, KV, G, d), 1, 0)

    def one(qc):
        s = jnp.einsum('bqkgd,blkd->bkgql', qc, k).astype(jnp.float32) * d ** -0.5
        if sink is not None:
            snk = jnp.broadcast_to(sink.astype(jnp.float32)[None, :, :, None, None], s.shape[:-1] + (1,))
            p = jax.nn.softmax(jnp.concatenate([s, snk], -1), -1)[..., :-1]
        else:
            p = jax.nn.softmax(s, -1)
        return jnp.einsum('bkgql,blkd->bqkgd', p.astype(v.dtype), v)

    o = lax.map(one, qb)
    return jnp.moveaxis(o, 0, 1).reshape(B, L, KV * G * d)

def window_attention_latent(q, k, v, k_ctx, v_ctx, sink):
    B, N, _, d = q.shape
    nb = N // WBLK
    lc = k_ctx.shape[1]
    qb = q.reshape(B, nb, WBLK, KV_B, G_B, d)
    pad = ((0, 0), (WBLK, WBLK), (0, 0), (0, 0))
    kp = jnp.pad(k, pad).reshape(B, nb + 2, WBLK, KV_B, d)
    vp = jnp.pad(v, pad).reshape(B, nb + 2, WBLK, KV_B, d)
    kband = jnp.concatenate([kp[:, :-2], kp[:, 1:-1], kp[:, 2:]], axis=2)
    vband = jnp.concatenate([vp[:, :-2], vp[:, 1:-1], vp[:, 2:]], axis=2)
    blk = jnp.arange(nb)
    kpos = blk[:, None] * WBLK - WBLK + jnp.arange(3 * WBLK)[None, :]
    qpos = blk[:, None] * WBLK + jnp.arange(WBLK)[None, :]
    mask = (jnp.abs(kpos[:, None, :] - qpos[:, :, None]) <= WIN) & (kpos[:, None, :] >= 0) & (kpos[:, None, :] < N)
    sink_l = sink.reshape(KV_B, G_B).astype(jnp.float32)
    scale = d ** -0.5

    def one(args):
        qc, kc, vc, mc = args
        s_loc = jnp.einsum('bqkgd,bskd->bkgqs', qc, kc).astype(jnp.float32) * scale
        s_loc = jnp.where(mc, s_loc, -jnp.inf)
        s_ctx = jnp.einsum('bqkgd,blkd->bkgql', qc, k_ctx).astype(jnp.float32) * scale
        snk = jnp.broadcast_to(sink_l[None, :, :, None, None], s_loc.shape[:-1] + (1,))
        p = jax.nn.softmax(jnp.concatenate([s_ctx, s_loc, snk], -1), -1).astype(v.dtype)
        return (jnp.einsum('bkgql,blkd->bqkgd', p[..., :lc], v_ctx)
                + jnp.einsum('bkgqs,bskd->bqkgd', p[..., lc:lc + 3 * WBLK], vc))

    o = lax.map(one, (jnp.moveaxis(qb, 1, 0), jnp.moveaxis(kband, 1, 0), jnp.moveaxis(vband, 1, 0), mask))
    return jnp.moveaxis(o, 0, 1).reshape(B, N, H_B * d)

def neighborhood_attention_latent(q, k, v, k_ctx, v_ctx, rpb_l):
    B, N, H, d = q.shape
    rows = N // GRID_W
    wh = min(NA_WIN_H, rows)
    ncb = GRID_W // NA_QCOL
    lc = k_ctx.shape[1]
    r = jnp.arange(rows)
    key_rows = jnp.clip(r - wh // 2, 0, rows - wh)[:, None] + jnp.arange(wh)[None, :]
    cb = jnp.arange(ncb)
    key_cols = jnp.clip(cb * NA_QCOL - NA_WIN_W // 2, 0, GRID_W - NA_KCOL)[:, None] + jnp.arange(NA_KCOL)[None, :]
    ri = key_rows[:, None, :, None]
    ci = key_cols[None, :, None, :]
    kg = k.reshape(B, rows, GRID_W, H, d)[:, ri, ci]
    vg = v.reshape(B, rows, GRID_W, H, d)[:, ri, ci]
    qg = q.reshape(B, rows, ncb, NA_QCOL, H, d)
    qcol = cb[:, None] * NA_QCOL + jnp.arange(NA_QCOL)[None, :]
    wstart = jnp.clip(qcol - NA_WIN_W // 2, 0, GRID_W - NA_WIN_W)
    kc3 = key_cols[:, None, :]
    in_win = (kc3 >= wstart[:, :, None]) & (kc3 < wstart[:, :, None] + NA_WIN_W)
    dr_idx = key_rows - r[:, None] + NA_WIN_H - 1
    dc_idx = jnp.clip(kc3 - qcol[:, :, None], 1 - NA_WIN_W, NA_WIN_W - 1) + NA_WIN_W - 1
    bias = rpb_l[:, dr_idx[:, None, None, :, None], dc_idx[None, :, :, None, :]].astype(jnp.float32)
    scale = d ** -0.5
    s_loc = jnp.einsum('brcqhd,brcwshd->bhrcqws', qg, kg).astype(jnp.float32) * scale + bias[None]
    s_loc = jnp.where(in_win[:, :, None, :], s_loc, -jnp.inf).reshape(B, H, rows, ncb, NA_QCOL, wh * NA_KCOL)
    s_ctx = jnp.einsum('brcqhd,blhd->bhrcql', qg, k_ctx).astype(jnp.float32) * scale
    p = jax.nn.softmax(jnp.concatenate([s_ctx, s_loc], -1), -1).astype(v.dtype)
    o = (jnp.einsum('bhrcql,blhd->brcqhd', p[..., :lc], v_ctx)
         + jnp.einsum('bhrcqws,brcwshd->brcqhd', p[..., lc:].reshape(B, H, rows, ncb, NA_QCOL, wh, NA_KCOL), vg))
    return o.reshape(B, N, H * d)

def moe_ffn(h, w_rg, w_re, w_g, w_u, w_d):
    shp = h.shape
    x = h.reshape(-1, shp[-1])
    T = x.shape[0]
    pg = jax.nn.softmax((x @ w_rg).astype(jnp.float32), -1)
    grp = jnp.argmax(pg, -1)
    g_w = jnp.max(pg, -1)
    le = (x @ w_re).astype(jnp.float32).reshape(T, N_GROUPS, E_PER_GROUP)
    le = jnp.take_along_axis(le, grp[:, None, None], axis=1)[:, 0]
    top_l, top_i = lax.top_k(le, TOP_K)
    top_w = jax.nn.softmax(top_l, -1) * g_w[:, None]
    e_flat = (grp[:, None] * E_PER_GROUP + top_i).reshape(-1)
    w_flat = top_w.reshape(-1)
    t_flat = jnp.repeat(jnp.arange(T), TOP_K)
    A = T * TOP_K
    order = jnp.argsort(e_flat)
    e_s, t_s, w_s = e_flat[order], t_flat[order], w_flat[order]
    counts = jnp.bincount(e_flat, length=N_EXPERTS)
    start = jnp.cumsum(counts) - counts
    padded = (counts + MOE_BLK - 1) // MOE_BLK * MOE_BLK
    p_end = jnp.cumsum(padded)
    p_start = p_end - padded
    pos = p_start[e_s] + jnp.arange(A) - start[e_s]
    nblk = -(-A // MOE_BLK) + N_EXPERTS
    buf = jnp.zeros((nblk * MOE_BLK, x.shape[-1]), x.dtype).at[pos].set(x[t_s])
    blk_e = jnp.minimum(jnp.searchsorted(p_end, jnp.arange(nblk) * MOE_BLK, side='right'), N_EXPERTS - 1)

    def expert_block(args):
        xb, e = args
        return (jax.nn.silu(xb @ w_g[e]) * (xb @ w_u[e])) @ w_d[e]

    out = lax.map(expert_block, (buf.reshape(nblk, MOE_BLK, -1), blk_e)).reshape(nblk * MOE_BLK, -1)
    y = jax.ops.segment_sum(out[pos] * w_s[:, None].astype(out.dtype), t_s, num_segments=T)
    return y.reshape(shp)

def setup_inputs(seed: int = 0) -> dict:
    key = jax.random.key(seed)
    ks = jax.random.split(key, 28)

    def nrm(k, shape, s):
        return jax.random.normal(k, shape, jnp.float32) * s

    return {
        'x_prompt': nrm(ks[0], (BATCH, SEQ, D_MODEL), 1.0),
        'x_sample': nrm(ks[1], (DEC_BATCH, DEC_SEQ, D_MODEL), 1.0),
        'state_a_C': nrm(ks[2], (DEC_BATCH, DEPTH, 2, H_A, DH_A, DH_A), 0.5),
        'state_a_n': nrm(ks[3], (DEC_BATCH, DEPTH, 2, H_A, DH_A), 0.5),
        'state_a_m': nrm(ks[4], (DEC_BATCH, DEPTH, 2, H_A), 0.5),
        'cache_b_k': nrm(ks[5], (DEC_BATCH, DEPTH, PAST_LEN, KV_B, HD_B), 1.0),
        'cache_b_v': nrm(ks[6], (DEC_BATCH, DEPTH, PAST_LEN, KV_B, HD_B), 1.0),
        'cache_c_k': nrm(ks[7], (DEC_BATCH, DEPTH, PAST_LEN, H_C, HD_C), 1.0),
        'cache_c_v': nrm(ks[8], (DEC_BATCH, DEPTH, PAST_LEN, H_C, HD_C), 1.0),
        'c': nrm(ks[9], (DEC_BATCH, D_MODEL), 1.0),
        'c_ctx': nrm(ks[10], (D_MODEL,), 1.0),
        'w_in': nrm(ks[11], (DEPTH, D_MODEL, D_IN), D_MODEL ** -0.5),
        'b_a_i': nrm(ks[12], (DEPTH, 2, H_A), 0.1),
        'b_a_f': jnp.linspace(3.0, 6.0, H_A, dtype=jnp.float32)[None, None, :] + nrm(ks[13], (DEPTH, 2, H_A), 0.1),
        'w_a_hnorm': 1.0 + nrm(ks[14], (DEPTH, D_A), 0.02),
        'b_sink': nrm(ks[15], (DEPTH, H_B), 0.5),
        'rpb': nrm(ks[16], (DEPTH, H_C, 2 * NA_WIN_H - 1, 2 * NA_WIN_W - 1), 0.1),
        'w_out': nrm(ks[17], (DEPTH, D_MIX, D_MODEL), D_MIX ** -0.5 * BETA),
        'w_ada': nrm(ks[18], (DEPTH, D_MODEL, 6 * D_MODEL), 0.5 * D_MODEL ** -0.5),
        'b_ada': nrm(ks[19], (DEPTH, 6 * D_MODEL), 0.02),
        'ln_g': 1.0 + nrm(ks[20], (DEPTH, 2, D_MODEL), 0.02),
        'ln_b': nrm(ks[21], (DEPTH, 2, D_MODEL), 0.02),
        'w_router_grp': nrm(ks[22], (DEPTH, D_MODEL, N_GROUPS), D_MODEL ** -0.5),
        'w_router_exp': nrm(ks[23], (DEPTH, D_MODEL, N_EXPERTS), D_MODEL ** -0.5),
        'w_e_gate': nrm(ks[24], (DEPTH, N_EXPERTS, D_MODEL, D_EXPERT), D_MODEL ** -0.5),
        'w_e_up': nrm(ks[25], (DEPTH, N_EXPERTS, D_MODEL, D_EXPERT), D_MODEL ** -0.5),
        'w_e_down': nrm(ks[26], (DEPTH, N_EXPERTS, D_EXPERT, D_MODEL), D_EXPERT ** -0.5 * BETA),
    }

def reference(x_prompt, x_sample, state_a_C, state_a_n, state_a_m, cache_b_k, cache_b_v, cache_c_k, cache_c_v,
              c, c_ctx, w_in, b_a_i, b_a_f, w_a_hnorm, b_sink, rpb, w_out, w_ada, b_ada, ln_g, ln_b,
              w_router_grp, w_router_exp, w_e_gate, w_e_up, w_e_down):
    x = x_prompt
    B, L, _ = x.shape
    zC = jnp.zeros((B, 2, H_A, DH_A, DH_A), jnp.float32)
    zn = jnp.zeros((B, 2, H_A, DH_A), jnp.float32)
    zm = jnp.zeros((B, 2, H_A), jnp.float32)
    Cs, ns, ms, kbs, vbs, kcs, vcs = [], [], [], [], [], [], []
    for l in range(DEPTH):
        sh_a, sc_a, g_a, sh_f, sc_f, g_f = adaln(c_ctx[None, :], w_ada[l], b_ada[l])
        h = x * (1.0 + sc_a) + sh_a
        qa, ka, va, oa, ia, fa, qb, kb, vb, qc, kc, vc = split_proj(h @ w_in[l])
        ya, Cl, nl, ml = mlstm_mixer(qa, ka, va, oa, ia, fa, b_a_i[l], b_a_f[l], w_a_hnorm[l], zC, zn, zm)
        kb4 = kb.reshape(B, L, KV_B, HD_B)
        vb4 = vb.reshape(B, L, KV_B, HD_B)
        yb = ctx_attention(qb.reshape(B, L, KV_B, G_B, HD_B), kb4, vb4, b_sink[l].reshape(KV_B, G_B))
        kc4 = kc.reshape(B, L, H_C, HD_C)
        vc4 = vc.reshape(B, L, H_C, HD_C)
        yc = ctx_attention(qc.reshape(B, L, H_C, 1, HD_C), kc4, vc4, None)
        x = post_norm(x, jnp.concatenate([ya, yb, yc], -1) @ w_out[l], g_a, ln_g[l, 0], ln_b[l, 0])
        h = x * (1.0 + sc_f) + sh_f
        x = post_norm(x, moe_ffn(h, w_router_grp[l], w_router_exp[l], w_e_gate[l], w_e_up[l], w_e_down[l]), g_f, ln_g[l, 1], ln_b[l, 1])
        Cs.append(Cl); ns.append(nl); ms.append(ml)
        kbs.append(kb4); vbs.append(vb4); kcs.append(kc4); vcs.append(vc4)
    y_prompt = x

    x = x_sample
    Bd, N, _ = x.shape
    cos, sin = axial_rope(N, HD_B)
    for l in range(DEPTH):
        sh_a, sc_a, g_a, sh_f, sc_f, g_f = adaln(c, w_ada[l], b_ada[l])
        h = x * (1.0 + sc_a) + sh_a
        qa, ka, va, oa, ia, fa, qb, kb, vb, qc, kc, vc = split_proj(h @ w_in[l])
        ya, _, _, _ = mlstm_mixer(qa, ka, va, oa, ia, fa, b_a_i[l], b_a_f[l], w_a_hnorm[l],
                                  state_a_C[:, l], state_a_n[:, l], state_a_m[:, l])
        qb4 = apply_rope(qb.reshape(Bd, N, H_B, HD_B), cos, sin)
        kb4 = apply_rope(kb.reshape(Bd, N, KV_B, HD_B), cos, sin)
        yb = window_attention_latent(qb4, kb4, vb.reshape(Bd, N, KV_B, HD_B), cache_b_k[:, l], cache_b_v[:, l], b_sink[l])
        yc = neighborhood_attention_latent(qc.reshape(Bd, N, H_C, HD_C), kc.reshape(Bd, N, H_C, HD_C),
                                           vc.reshape(Bd, N, H_C, HD_C), cache_c_k[:, l], cache_c_v[:, l], rpb[l])
        x = post_norm(x, jnp.concatenate([ya, yb, yc], -1) @ w_out[l], g_a, ln_g[l, 0], ln_b[l, 0])
        h = x * (1.0 + sc_f) + sh_f
        x = post_norm(x, moe_ffn(h, w_router_grp[l], w_router_exp[l], w_e_gate[l], w_e_up[l], w_e_down[l]), g_f, ln_g[l, 1], ln_b[l, 1])
    y_sample = x

    new_state_a_C = jnp.stack(Cs, 1)
    new_state_a_n = jnp.stack(ns, 1)
    new_state_a_m = jnp.stack(ms, 1)
    new_cache_b_k = jnp.stack(kbs, 1)
    new_cache_b_v = jnp.stack(vbs, 1)
    new_cache_c_k = jnp.stack(kcs, 1)
    new_cache_c_v = jnp.stack(vcs, 1)
    return (y_prompt, y_sample, new_state_a_C, new_state_a_n, new_state_a_m, new_cache_b_k, new_cache_b_v, new_cache_c_k, new_cache_c_v)


_drawn_inputs = setup_inputs


def setup_inputs(seed=0):
    import zlib

    import numpy as np

    out = dict(_drawn_inputs(seed))
    spreads = {}
    factors = {'state_a_C': 6.651,
     'state_a_n': 8.0,
     'state_a_m': 8.0,
     'cache_b_k': 8.0,
     'cache_b_v': 8.0,
     'cache_c_k': 8.0,
     'cache_c_v': 8.0,
     'w_a_hnorm': 44.663,
     'b_sink': 64.0,
     'rpb': 64.0}
    for name, (base, spread) in spreads.items():
        noise = np.random.default_rng([zlib.crc32(name.encode()), seed]).standard_normal(out[name].shape)
        drawn = base * np.exp(spread * noise) if base else spread * noise
        out[name] = __import__('jax').numpy.asarray(drawn.astype(out[name].dtype))
    for name, factor in factors.items():
        out[name] = (out[name] * factor).astype(out[name].dtype)
    return out
```

```python
from contextlib import ExitStack

import numpy as np
import concourse.bass as bass
from concourse import mybir

F32 = mybir.dt.float32
I32 = mybir.dt.int32
BF16 = mybir.dt.bfloat16
ALU = mybir.AluOpType
ACT = mybir.ActivationFunctionType
AX = mybir.AxisListType.X

P = 128
D = 1024
KD = D // P
SEQ, NLAT, DEPTH, PAST = 128, 512, 2, 128
NT = (SEQ + NLAT) // P
GRID_W, ROWS = 64, 8
HA, DA = 4, 96
HB, KVB, HC, HD = 6, 2, 4, 64
D_A, D_B, D_KVB, D_C = HA * DA, HB * HD, KVB * HD, HC * HD
D_IN = 4 * D_A + 4 * HA + D_B + 2 * D_KVB + 3 * D_C
C_QA, C_KA, C_VA, C_OA = 0, D_A, 2 * D_A, 3 * D_A
C_I = 4 * D_A
C_F = C_I + 2 * HA
C_QB = C_F + 2 * HA
C_KB = C_QB + D_B
C_VB = C_KB + D_KVB
C_QC = C_VB + D_KVB
C_KC = C_QC + D_C
C_VC = C_KC + D_C
NG, EPG, NE, DE = 4, 8, 32, 256
ALPHA = (2 * DEPTH) ** 0.25
EPS = 1e-5
NEG = -1.0e30
NTOK = NT * P
UN = 256
N_ADA, N_IN, N_OUT = 6 * D // UN, -(-D_IN // UN), D // UN
ADA0 = 2 * D // UN
RING = 6
BANKS = 7
MAXOVF = 2 * NTOK // P
NBLK = NE + MAXOVF
NLIST = NBLK + 2
FAR = 1 << 20
KS = [0, 8, 24, 32]
PAT = [0, 1, 1, 2]
OFFS = [0, -8, -16]
W97 = DA + 1

_C = {}
_c = 0
for _n, _w in (("ident", P), ("upper", P), ("lower", P), ("strict", P), ("ones", P), ("mneg_f", P), ("mneg_b", P),
               ("natmask", 3 * 32), ("cos", 4 * HD), ("sin", 4 * HD), ("sel", HA * P), ("io4", 4), ("io32", 32),
               ("eid", 32), ("io10", 10), ("half", 1), ("pm05", 1), ("csum", 2)):
    _C[_n] = (_c, _c + _w)
    _c += _w
NCONST = _c


def constants():
    c = np.zeros((P, NCONST), np.float32)

    def put(name, a):
        lo, hi = _C[name]
        c[:a.shape[0], lo:hi] = a.reshape(a.shape[0], -1)

    i = np.arange(P)
    up = (i[:, None] <= i[None, :]).astype(np.float32)
    put("ident", np.eye(P, dtype=np.float32))
    put("upper", up)
    put("lower", up.T)
    put("strict", (i[:, None] < i[None, :]).astype(np.float32))
    put("ones", np.ones((P, P), np.float32))
    put("mneg_f", np.where(up > 0, 0.0, NEG).astype(np.float32))
    put("mneg_b", np.where(up.T > 0, 0.0, NEG).astype(np.float32))
    nat = np.zeros((P, 3, 32), np.float32)
    qc = 15 - np.arange(P) % 16
    for p, (cb, ks) in enumerate(((0, 0), (1, 8), (3, 32))):
        col = cb * 16 + qc
        w0 = np.clip(col - 8, 0, GRID_W - 16)
        kc = ks + np.arange(32)
        ok = (kc[None, :] >= w0[:, None]) & (kc[None, :] < w0[:, None] + 16)
        nat[:, p] = np.where(ok, 0.0, NEG)
    put("natmask", nat)
    tok = np.arange(NLAT).reshape(4, P).T
    nf = HD // 4
    inv = (np.float32(10000.0) ** (-np.arange(nf, dtype=np.float32) / np.float32(nf))).astype(np.float32)
    ar = (tok // GRID_W).astype(np.float32)[..., None] * inv
    ac = (tok % GRID_W).astype(np.float32)[..., None] * inv
    ang = np.concatenate([ar, ar, ac, ac], -1)
    sin = np.sin(ang).astype(np.float32)
    sin[..., 0:nf] *= -1
    sin[..., 2 * nf:3 * nf] *= -1
    put("cos", np.cos(ang).astype(np.float32))
    put("sin", sin)
    sel = np.zeros((36, HA, P), np.float32)
    for h in range(HA):
        sel[h, h] = sel[32 + h, h] = 1.0
    put("sel", sel)
    row = lambda a: np.broadcast_to(np.asarray(a, np.float32), (P, len(a))).copy()
    put("io4", row(4 - np.arange(4)))
    put("io32", row(32 - np.arange(32)))
    put("eid", row(np.arange(32)))
    put("io10", row(np.arange(10)))
    put("half", row([0.5]))
    put("csum", np.tile(np.eye(32, 2, dtype=np.float32), (4, 1)))
    put("pm05", row([-0.5]))
    return c


FILL2 = 17


class Count:

    def __init__(self, reg, times, plus):
        self.reg, self.times, self.plus = reg, times, plus

    def __mul__(self, k):
        return Count(self.reg, self.times * k, self.plus * k)

    def __add__(self, k):
        return Count(self.reg, self.times, self.plus + k)

    def __sub__(self, k):
        return self + (-k)


def now(value):
    return value if isinstance(value, int) else value.reg * value.times + value.plus


STAGE = {}
for _stage, _steps in (
        ("cond", ("sig_c", "silu_c", "maskb", "modT", "arow", "acol")),
        ("gates", ("g_ln", "g_na", "gates", "brow", "mp_zero", "emo", "scin", "mp")),
        ("mlstm", ("w", "mo", "wkv", "qts", "A_done", "hcent", "hsq", "osig", "hvar", "hrstd", "hnorm", "v1", "A_out")),
        ("attn", ("esink", "negmax", "biased", "rope_half", "rope", "vp", "bias")),
        ("norm", ("lnhat", "lnvar", "lnnm", "lng", "lnrstd", "x1", "x2", "hsc", "h2", "comb")),
        ("route", ("r_ge", "r_ed", "r_gd", "r_dl", "assign", "slots", "ctl", "listf"))):
    for _step in _steps:
        STAGE[_step] = _stage


def above_zero(value):
    return not isinstance(value, int) or value > 0


class Events:

    def __init__(self, table):
        self.known, self.table, self.count, self.sems = table, {}, {}, {}

    def open(self, ctx, nc):
        self.ctx, self.nc = ctx, nc

    def sem(self, name):
        if name not in self.sems:
            self.sems[name] = self.ctx.enter_context(self.nc.semaphore(name))
        return self.sems[name]

    def event(self, name, key, by=1):
        self.count[name] = self.count.get(name, 0) + by
        self.table[key] = (name, self.count[name])
        return self.sem(name), by

    def at(self, *key):
        if key not in self.known:
            assert not self.known, key
            return self.sem("unit_used"), 1
        name, value = self.known[key]
        return self.sem(name), value


class Engine:

    def __init__(self, ev, name):
        self.ev, self.name, self.newest = ev, name, None

    def event(self, *key, by=1, sem=None):
        if sem is None:
            sem = str(key[0]) if by > 1 else f"{self.name}_{STAGE.get(key[0], key[0])}"
        out = self.ev.event(sem, key, by)
        self.newest = self.ev.table[key]
        return out

    def step(self):
        return self.event(self.name, "step", self.ev.count.get(self.name + "_step", 0), sem=self.name + "_step")

    def last(self):
        name, value = self.newest
        return self.ev.sem(name), value


class Jobs:

    def __init__(self, ev, psum):
        self.ev, self.psum, self.n = ev, psum, 0

    def open(self, *key):
        self.ev.table[("job",) + key] = self.n
        self.n += 1
        return self.psum[(self.n - 1) % BANKS]

    def room(self):
        n = self.n - 1
        return self.ev.at("free", n - BANKS) if n >= BANKS else self.ev.at("silu_c")

    def filled(self):
        n = self.n - 1
        return self.ev.event(f"bank_full{n % BANKS}", ("full", n))

    def number(self, key):
        return self.ev.table.get(("job",) + key, self.ev.known.get(("job",) + key, 0))

    def bank(self, *key):
        return self.psum[self.number(key) % BANKS]

    def full(self, *key):
        return self.ev.at("full", self.number(key))

    def freed(self, *key):
        n = self.number(key)
        name = f"bank_free{n % BANKS}"
        self.ev.table[("free", n)] = (name, n // BANKS + 1)
        return self.ev.sem(name), 1

    def empty(self, *key):
        return self.ev.at("free", self.number(key))


STEPS_P = [((0, 0), (1, 0))]
STEPS_S = [((0, 1 + s), (1, 4 - s)) for s in range(4)]
STEPS = STEPS_P + STEPS_S


def b_units():
    return [(t, h) for t in range(NT) for h in range(HB)]


def c_units():
    return [(t, h) for t in range(NT) for h in range(HC)]


def b_keys(t):
    if t == 0:
        return None
    s = t - 1
    lo, hi = max(0, s - 1), min(3, s + 1)
    return lo, hi - lo + 1


def program(nc, A, table):
    ev = Events(table)
    with ExitStack() as ctx:
        ev.open(ctx, nc)
        sb = lambda n, s, d=F32: ctx.enter_context(nc.sbuf_tensor(n, s, d))
        dram = lambda n, s, d=F32: nc.dram_tensor(n, s, d).ap()

        x = sb("x", [P, NT, D])
        hT = sb("hT", [P, KD * NTOK])
        z = sb("z", [P, NT * D_IN])
        ring = sb("ring", [P, RING, KD * UN])
        att = sb("att", [P, 11400])
        const = sb("const", [P, NCONST])
        identb = sb("identb", [P, P], BF16)
        maskb = sb("maskb", [P, 2, P], BF16)
        cs = sb("cs", [P, 2, KD, 2])
        cond = sb("cond", [P, KD, 32])
        arow = sb("arow", [P, UN])
        modr = arow[0:32, :].rearrange("p (g n) -> p g n", g=2)
        modT = sb("modT", [P, 2, 48])
        bada = sb("bada", [P, DEPTH, 48])
        wr = sb("wr", [P, KD, 36])
        gb = sb("gb", [P, 16])
        sinkt = sb("sinkt", [P, 2, HB])
        small = sb("small", [P, 260])
        ids = sb("ids", [P, 2 * NT], I32)
        sidx = sb("sidx", [P, NLIST], I32)
        gidx = sb("gidx", [P, NLIST], I32)
        cur = sb("cur", [P, 4], I32)
        ctl = sb("ctl", [1, 16], I32)

        mod_dram = [dram(f"mod_rows{l}", [2, 32, P]) for l in range(DEPTH)]
        h2_dram = [dram(f"h2_rows{l}", [NTOK, D]) for l in range(DEPTH)]
        y_dram = [dram(f"expert_rows{l}", [2 * NTOK, D]) for l in range(DEPTH)]
        list_dram = [dram(f"slot_list{l}", [NLIST * P, 1], I32) for l in range(DEPTH)]
        shift_dram = [dram(f"bias_shifted{l}", [3, 16, HC, 15, 32]) for l in range(DEPTH)]
        bias_dram = [dram(f"bias_full{l}", [3, P, HC, 256]) for l in range(DEPTH)]

        bank = [ctx.enter_context(nc.psum_tensor(f"bank{b}", [P, 512], F32)) for b in range(8)]
        jobs = Jobs(ev, bank)
        ada_ps = bank[7]

        K = {n: const[:, lo:hi] for n, (lo, hi) in _C.items()}
        ident = K["ident"]
        hTv = hT[:, :].rearrange("p (k n) -> p k n", k=KD)
        zv = z[:, :].rearrange("p (t n) -> p t n", t=NT)

        def region(t, off, parts, *shape):
            n = 1
            for s in shape:
                n *= s
            a = t[0:parts, off:off + n]
            if len(shape) == 2:
                a = a.rearrange("p (a b) -> p a b", a=shape[0])
            if len(shape) == 3:
                a = a.rearrange("p (a b c) -> p a b c", a=shape[0], b=shape[1])
            if len(shape) == 4:
                a = a.rearrange("p (a b c d) -> p a b c d", a=shape[0], b=shape[1], c=shape[2])
            return a

        def layout(t, start, parts):
            out, at = {}, start
            for name, p, *shape in parts:
                out[name] = region(t, at, p, *shape)
                n = 1
                for s in shape:
                    n *= s
                at += n
            assert at <= t.shape[1], (at, t.shape)
            return out

        qkA = region(hT, 0, DA, 2, HA, NTOK)
        a = layout(att, 0, [
            ("v1", P, NT, HA, W97), ("gi", P, NT, 36), ("gf", P, NT, 36), ("gbk", P, NT, 36),
            ("brow", 36, NTOK), ("grow", 36, NTOK), ("gmax", 36, NTOK), ("emo", 36, NTOK), ("scin", 36, NTOK),
            ("gc", P, NT, 72), ("CT", DA, 2, HA, W97), ("wt", P, 2, HA, P), ("qts", DA, 2, HA, P),
            ("wkv", P, 2, HA, W97), ("si", W97, 8, DA), ("hn", P, D_A), ("rope", P, 2, 256)])
        sq = region(att, 0, P, NT, D_A)
        b = layout(hT, 0, [("kT", HD, KVB, 768), ("qT", HD, 2, HB, P), ("vp", P, 4, 2, D_C)])
        c = layout(att, 1920, [
            ("kT", HD, HC, 768), ("qT", HD, HC, NTOK), ("p", P, 3, 512), ("pT", P, 2, 512),
            ("bk", P, D_KVB), ("bv", P, D_KVB), ("bt", P, 2, 256), ("ck", P, D_C), ("cv", P, D_C)])
        m = layout(z, 0, [
            ("ga", P, 2, D), ("ln", P, 2, D), ("scsh", P, 2, 2, D), ("gf", P, 2, D), ("hs", P, 2, D), ("h2T", P, KD, P)])
        o12 = region(z, 4096, P, 2, 2, D)
        e = layout(att, 0, [
            ("xg", P, 2, D), ("xT", P, 2, D), ("sig", P, 2, DE), ("hm", P, 2, DE), ("hmT", P, 2, 2 * P), ("ob", P, 2, D),
            ("tmp", P, 512)])
        r = layout(att, 8300, [
            ("lg", P, NT, 36), ("e1", P, NT, NE), ("e2", P, NT, NE), ("ma", P, NT, NE), ("rk", P, 6, NE),
            ("t1", P, NT, NE), ("t2", P, NT, NE), ("lem", P, NT, NE), ("lf", NLIST, P), ("ov", P, 10, NE)])
        s5 = region(small, 0, P, 20, NT)
        stats = region(small, 100, P, 2, 6)
        lnv = sb("lnv", [P, NT, 8])
        nrm = region(small, 120, P, 100)
        w12 = region(small, 220, P, 2, NT)
        mp = region(small, 230, 36, 6)
        scs = region(small, 236, DA, 2, HA)
        den = region(small, 244, P, 2, HA)
        ctlf = sb("ctlf", [1, 16])[:, :]
        htmp = sb("htmp", [P, D_A])
        posi = sb("posi", [P, 2 * NT], I32)
        listi = htmp[0:NLIST, 0:P].bitcast(I32)
        flist = arow[0:NLIST, 0:P].bitcast(I32)
        sm = sb("sm", [P, 3, 64])
        hst = sb("hst", [P, 4, 20])


        def bc(ap, axis, n):
            u = ap.unsqueeze(axis)
            shape = list(u.shape)
            shape[axis] = n
            return u.broadcast_to(shape)

        order = []
        for l in range(DEPTH):
            todo = [(l, "ada", i) for i in range(ADA0)] if l == 0 else []
            todo += [(l, "in", i) for i in range(N_IN)] + [(l, "ada", i) for i in range(ADA0, N_ADA)]
            if l + 1 < DEPTH:
                todo += [(l + 1, "ada", i) for i in range(ADA0)]
            todo += [(l, "out", i) for i in range(N_OUT)]
            order.append(todo)
        slot_of, uses = {}, [0] * RING
        for todo in order:
            for n, u in enumerate(todo):
                uses[n % RING] += 1
                slot_of[u] = (n % RING, uses[n % RING])
        ring_full = [ev.sem(f"ring_full{s}") for s in range(RING)]

        MOE = [{n: ev.sem(f"{n}_{l}") for n in (
            "gath0", "gath1", "xT_psum", "xT_act", "xT_dve", "gu", "sig", "hm_part", "hm", "hT_psum", "hT",
            "out_psum", "out_act", "out_dve", "scat0", "scat1", "cur_gath", "cur_scat",
            "w0", "w1", "w2", "w3", "w4", "w5")} for l in range(DEPTH)]

        def turns(eng, l, body):
            body(0)
            body(1)
            eng.wait_ge(*ev.at("ctl", l))
            more = eng.value_load(ctl[0:1, 12:13], min_val=NE // 2 - 2, max_val=NBLK // 2 - 2)
            with eng.Fori(0, more) as i:
                body(Count(i, 1, 2))
            return Count(more, 1, 2)

        def b_ctx_k(kv):
            return c["bk"][:, kv * HD:(kv + 1) * HD]

        def attention_units():
            return [("B", t, h) for t, h in b_units()] + [("C", t, h) for t, h in c_units()]

        def n_keys(unit):
            kind, t, _ = unit
            if t == 0:
                return 1
            return 1 + b_keys(t)[1] if kind == "B" else 3

        def mix_cols(t, k):
            at = C_QA + k * P if k < 3 else C_QB + (k - 3) * P if k < 6 else C_QC + (k - 6) * P
            return zv[:, t, at:at + P]

        def z_out(n, g):
            t0 = 2 * g
            cnt = min(2, NT - t0)
            nw = min(UN, D_IN - n * UN)
            return cnt, nw, zv[:, t0:t0 + cnt, n * UN:n * UN + nw]

        def x_mix_out(k, bk):
            if k < 6:
                return hTv[:, k, P:NTOK], bk[:, :]
            o = hTv[:, k, P:NTOK].rearrange("p (r b c) -> p b r c", r=ROWS, b=4)
            return o, bk[:, :].rearrange("p (b r c) -> p b r c", b=4, r=ROWS)[:, :, :, ::-1]

        block = ctx.enter_context(nc.Block())

        @block.sync
        def _(eng):
            sp = Engine(ev, "sp")

            def ld(dst, src, *key):
                eng.dma_start(dst, src).then_inc(*sp.event(*key, by=16, sem="_".join(map(str, key))))

            ld(const[:, :], A["const"], "ld_const")
            ld(cs[:, 0, :, :].rearrange("p k g -> p (k g)"), A["c_T"], "ld_c")
            ld(bada[:, :, :].rearrange("p l n -> p (l n)"), A["bada_T"], "ld_bada")
            holder = {}
            for l in range(DEPTH):
                for u in order[l]:
                    if l == 0 and u == (0, "ada", RING):
                        for t in range(NT):
                            ld(x[:, t, :], A["x_all"][t * P:(t + 1) * P, :], "ld_x", t)
                    s = slot_of[u][0]
                    if s in holder:
                        eng.wait_ge(*ev.at(*holder[s]))
                    eng.dma_start(ring[:, s, :], A["w_" + u[1]][u[0], u[2]]).then_inc(ring_full[s], 16)
                    holder[s] = ("unit_used",) + u
                W = MOE[l]

                def expert_units(ex, j, i):
                    for q in range(3):
                        if i is not None:
                            if above_zero(i * 2 + (j - 1)):
                                eng.wait_ge(W["gu"] if q < 2 else W["out_psum"], now(i * 2 + (j - 1)))
                        src = A["w_exp"][l, ex, q] if isinstance(ex, int) else \
                            A["w_exp"][l, bass.ds(ex, 1), q].rearrange("o p n -> p (o n)")
                        eng.dma_start(ring[:, 3 * j + q, :], src).then_inc(W[f"w{3 * j + q}"], 16)

                for j in range(2):
                    for q in range(3):
                        eng.wait_ge(*ev.at(*holder[3 * j + q]))
                    expert_units(j, j, None)
                with eng.Fori(0, NE // 2 - 2) as i:
                    for j in range(2):
                        expert_units(i * 2 + (2 + j), j, Count(i, 1, 1))
                eng.wait_ge(*ev.at("ctl", l))
                more = eng.value_load(ctl[0:1, 13:14], min_val=1, max_val=NBLK // 2 - NE // 2 + 1)
                with eng.Fori(0, more) as i:
                    for j in range(2):
                        ex = eng.value_load(ctl[0:1, bass.ds(i * 2 + j, 1)], min_val=0, max_val=NE - 1)
                        expert_units(ex, j, Count(i, 1, NE // 2 - 1))
                eng.wait_ge(W["out_psum"], more * 2 + (NE - 2))
                holder = {}
            for t in range(NT):
                eng.wait_ge(*ev.at("x2", DEPTH - 1, t))
                dst = A["y_prompt"][0] if t == 0 else A["y_sample"][0, (t - 1) * P:t * P, :]
                ld(dst, x[:, t, :], "st_y", t)
            for t in range(NT):
                eng.wait_ge(*ev.at("st_y", t))

        @block.tensor
        def _(eng):
            pe = Engine(ev, "pe")

            def unit_view(u):
                s, n = slot_of[u]
                eng.wait_ge(ring_full[s], 16 * n)
                return ring[:, s, :].rearrange("p (k n) -> p k n", k=KD)

            def job(ins, *key):
                ins.then_inc(*jobs.filled())

            ada_open = []

            def ada_rows(l, u):
                w = unit_view((l, "ada", u))
                if ada_done:
                    eng.wait_ge(*ev.at("arow", *ada_done[-1]))
                for kk in range(2):
                    for j in range(4):
                        last = eng.matmul(ada_ps[32 * j:32 * j + 32, P:P + UN], cond[:, 2 * j + kk, :],
                                          w[:, 2 * j + kk, :], start=(kk == 0), stop=(kk == 1))
                last.then_inc(*pe.event("unit_used", l, "ada", u))
                ada_done.append((l, u))
                ada_open.append((l, u))

            def ada_cols():
                l, u = ada_open.pop(0)
                eng.wait_ge(*ev.at("arow", l, u))
                if u == 0 and l > 0:
                    eng.wait_ge(*ev.at("modT", l - 1, 1))
                for i in range(2):
                    ch = 2 * u + i
                    last = eng.matmul(ada_ps[:, 2 * ch:2 * ch + 2], arow[:, i * P:(i + 1) * P], K["csum"],
                                      start=True, stop=True)
                last.then_inc(*pe.event("acol", l, u))

            def ada_unit(l, u):
                ada_rows(l, u)
                if len(ada_open) > 1:
                    ada_cols()

            ada_done = []
            eng.wait_ge(*ev.at("ld_const"))
            eng.wait_ge(*ev.at("silu_c"))
            for u in range(ADA0):
                ada_unit(0, u)
            ada_cols()
            for l in range(DEPTH):
                fill1 = [(l, u) for u in range(ADA0, N_ADA)]
                fill2 = [(l + 1, u) for u in range(ADA0)] if l + 1 < DEPTH else []

                def fill(todo, n):
                    for _ in range(min(n, len(todo))):
                        ada_unit(*todo.pop(0))

                for k in range(KD):
                    bk = jobs.open("H", l, k)
                    eng.wait_ge(*jobs.room())
                    for t in range(1, NT):
                        if k == 0:
                            eng.wait_ge(*ev.at(*(("ld_x", t) if l == 0 else ("x2", l - 1, t))))
                        last = eng.transpose(bk[:, (t - 1) * P:t * P], x[:, t, k * P:(k + 1) * P], ident)
                    last.then_inc(*jobs.filled())
                for j in range(2):
                    bk = jobs.open("Hp", l, j)
                    eng.wait_ge(*jobs.room())
                    eng.wait_ge(*ev.at(*(("ld_x", 0) if l == 0 else ("x2", l - 1, 0))))
                    for k in range(4):
                        last = eng.transpose(bk[:, k * P:(k + 1) * P], x[:, 0, (4 * j + k) * P:(4 * j + k + 1) * P], ident)
                    last.then_inc(*jobs.filled())
                for k in range(KD):
                    eng.wait_ge(*jobs.empty("H", l, k))
                for j in range(2):
                    eng.wait_ge(*jobs.empty("Hp", l, j))
                for n in range(N_IN):
                    w = unit_view((l, "in", n))
                    nw = min(UN, D_IN - n * UN)
                    for g in range(3):
                        bk = jobs.open("Z", l, n, g)
                        eng.wait_ge(*jobs.room())
                        for i, t in enumerate(range(2 * g, min(2 * g + 2, NT))):
                            for k in range(KD):
                                last = eng.matmul(bk[:, i * UN:i * UN + nw], hTv[:, k, t * P:(t + 1) * P],
                                                  w[:, k, 0:nw], start=(k == 0), stop=(k == KD - 1))
                        last.then_inc(*jobs.filled())
                    ev.table[("unit_used", l, "in", n)] = ev.table[("full", jobs.n - 1)]

                for t in range(NT):
                    bk = jobs.open("AG", l, t)
                    eng.wait_ge(*jobs.room())
                    eng.wait_ge(*ev.at("gates", l))
                    eng.matmul(bk[0:36, 0:P], a["gi"][:, t, :], ident, start=True, stop=True)
                    eng.matmul(bk[0:36, P:2 * P], a["gf"][:, t, :], K["upper"], start=True, stop=False)
                    last = eng.matmul(bk[0:36, P:2 * P], a["gbk"][:, t, :], K["lower"], start=False, stop=True)
                    last.then_inc(*jobs.filled())
                for t in range(NT):
                    for q, col in (("AQ", C_QA), ("AK", C_KA)):
                        bk = jobs.open(q, l, t)
                        eng.wait_ge(*jobs.room())
                        if t == 0:
                            for n in range(-(-(C_KA + D_A) // UN)):
                                for g in range(3):
                                    eng.wait_ge(*jobs.empty("Z", l, n, g))
                        for h in range(HA):
                            last = eng.transpose(bk[0:DA, h * P:(h + 1) * P],
                                                 zv[:, t, col + h * DA:col + (h + 1) * DA], ident)
                        last.then_inc(*jobs.filled())
                for d in range(2):
                    bk = jobs.open("AS", l, d)
                    eng.wait_ge(*jobs.room())
                    eng.wait_ge(*ev.at("ld_si", l))
                    for h in range(HA):
                        last = eng.transpose(bk[0:DA, h * W97:(h + 1) * W97], a["si"][:, d * HA + h, :],
                                             ident[0:W97, 0:W97])
                    last.then_inc(*jobs.filled())
                fill(fill1, 2)
                bk = jobs.open("AC", l)
                eng.wait_ge(*jobs.room())
                for t in range(NT):
                    eng.wait_ge(*jobs.empty("AG", l, t))
                eng.wait_ge(*ev.at("emo", l))
                for t in range(NT):
                    for i, rows in enumerate((a["grow"], a["emo"])):
                        last = eng.transpose(bk[:, t * 72 + i * 36:t * 72 + i * 36 + 36],
                                             rows[:, t * P:(t + 1) * P], ident[0:36, 0:36])
                last.then_inc(*jobs.filled())
                eng.wait_ge(*ev.at("scin", l))
                for si, pair in enumerate(STEPS):
                    for d, t in pair:
                        lo = 32 * d
                        tc = slice(t * P, (t + 1) * P)
                        for q, rows, m_ in (("AB", a["gmax"], P), ("AI", a["scin"], DA)):
                            bk = jobs.open(q, l, d, t)
                            eng.wait_ge(*jobs.room())
                            for h in range(HA):
                                last = eng.matmul(bk[0:m_, h * P:(h + 1) * P],
                                                  K["sel"][lo:lo + HA, h * P:h * P + m_],
                                                  rows[lo:lo + HA, tc], start=True, stop=True)
                            last.then_inc(*jobs.filled())
                        bk = jobs.open("AT", l, d, t)
                        eng.wait_ge(*jobs.room())
                        eng.wait_ge(*jobs.empty("AQ", l, t))
                        eng.wait_ge(*jobs.empty("AK", l, t))
                        for h in range(HA):
                            last = eng.matmul(bk[:, h * P:(h + 1) * P], qkA[:, 1, h, tc], qkA[:, 0, h, tc],
                                              start=True, stop=True)
                        last.then_inc(*jobs.filled())
                    fill(fill1, 3)
                    for d, t in pair:
                        bk = jobs.open("AN", l, d, t)
                        eng.wait_ge(*jobs.room())
                        eng.wait_ge(*ev.at("v1", l))
                        eng.wait_ge(*ev.at("sw", l, d, t))
                        if si == 1:
                            eng.wait_ge(*jobs.empty("AS", l, d))
                        if si > 0:
                            eng.wait_ge(*ev.at("qts", l, d, t))
                        if si > 1:
                            eng.wait_ge(*ev.at("CT", l, d, t))
                        for h in range(HA):
                            last = eng.matmul(bk[:, h * W97:(h + 1) * W97], a["wt"][:, d, h, :], a["v1"][:, t, h, :],
                                              start=True, stop=(t == 0))
                            if t > 0:
                                last = eng.matmul(bk[:, h * W97:(h + 1) * W97], a["qts"][:, d, h, :],
                                                  a["CT"][:, d, h, :], start=False, stop=True)
                        last.then_inc(*jobs.filled())
                        if si < len(STEPS) - 1:
                            bk = jobs.open("AU", l, d, t)
                            eng.wait_ge(*jobs.room())
                            eng.wait_ge(*ev.at("wkv", l, d, t))
                            for h in range(HA):
                                kz = zv[:, t, C_KA + h * DA:C_KA + (h + 1) * DA]
                                if t == 0:
                                    last = eng.matmul(bk[0:W97, h * DA:(h + 1) * DA], a["wkv"][:, d, h, :], kz,
                                                      start=True, stop=True)
                                else:
                                    last = eng.matmul(bk[0:DA, h * W97:(h + 1) * W97], kz, a["wkv"][:, d, h, :],
                                                      start=True, stop=True)
                            last.then_inc(*jobs.filled())
                fill(fill1, 99)
                ada_cols()
                bk = jobs.open("MR", l)
                eng.wait_ge(*jobs.room())
                eng.wait_ge(*ev.at("modT", l, 1))
                for g in range(2):
                    last = eng.transpose(bk[0:32, g * P:(g + 1) * P], modT[:, g, 16:48], ident)
                last.then_inc(*jobs.filled())

                for j, tiles in enumerate(((1, 2), (3, 4), (0, None))):
                    bk = jobs.open("BK", l, j)
                    eng.wait_ge(*jobs.room())
                    eng.wait_ge(*ev.at("A_done", l))
                    for n in range(N_IN):
                        for g in range(3):
                            eng.wait_ge(*jobs.empty("Z", l, n, g))
                    for t in range(1, NT):
                        eng.wait_ge(*ev.at("rope", l, t))
                    for i, t in enumerate(tiles):
                        if t is None:
                            eng.wait_ge(*ev.at("ld_cache", l))
                        for kv in range(KVB):
                            src = b_ctx_k(kv) if t is None else zv[:, t, C_KB + kv * HD:C_KB + (kv + 1) * HD]
                            last = eng.transpose(bk[0:HD, (2 * i + kv) * P:(2 * i + kv + 1) * P], src, ident)
                    last.then_inc(*jobs.filled())
                U = attention_units()

                def scores(u):
                    kind, t, h = U[u]
                    if kind == "B" and h == 0:
                        for j, hs in enumerate(((0, 1, 2, 3), (4, 5))):
                            bk = jobs.open("BQ", l, t, j)
                            eng.wait_ge(*jobs.room())
                            for i, hh in enumerate(hs):
                                last = eng.transpose(bk[0:HD, i * P:(i + 1) * P],
                                                     zv[:, t, C_QB + hh * HD:C_QB + (hh + 1) * HD], ident)
                            last.then_inc(*jobs.filled())
                    if kind == "C" and (t, h) == (0, 0):
                        for tt in range(NT + 1):
                            for q, col in (("CK", C_KC), ("CQ", C_QC)):
                                if tt == NT and q == "CQ":
                                    continue
                                bk = jobs.open(q, l, tt)
                                eng.wait_ge(*jobs.room())
                                for hh in range(HC):
                                    src = c["ck"][:, hh * HD:(hh + 1) * HD] if tt == NT else \
                                        zv[:, tt, col + hh * HD:col + (hh + 1) * HD]
                                    last = eng.transpose(bk[0:HD, hh * P:(hh + 1) * P], src, ident)
                                last.then_inc(*jobs.filled())
                    bk = jobs.open("S", l, u)
                    eng.wait_ge(*jobs.room())
                    if kind == "B":
                        eng.wait_ge(*jobs.empty("BQ", l, t, 0))
                        eng.wait_ge(*jobs.empty("BQ", l, t, 1))
                        for j in range(3):
                            eng.wait_ge(*jobs.empty("BK", l, j))
                        q = b["qT"][:, t % 2, h, :]
                        kT = b["kT"][:, h // (HB // KVB), :]
                        if t == 0:
                            last = eng.matmul(bk[:, 0:P], q, kT[:, 640:768], start=True, stop=True)
                        else:
                            lo, nl = b_keys(t)
                            eng.matmul(bk[:, 0:P], q, kT[:, 0:P], start=True, stop=True)
                            eng.matmul(bk[:, P:P + nl * P], q, kT[:, P + lo * P:P + (lo + nl) * P],
                                       start=True, stop=False, skip_group_check=True)
                            edges = ([(0, P)] if t > 1 else []) + ([(1, nl * P)] if t < NT - 1 else [])
                            for which, at in edges:
                                last = eng.matmul(bk[:, at:at + P], identb[:, :], maskb[:, which, :], start=False,
                                                  stop=(at == edges[-1][1]), skip_group_check=True)
                    else:
                        for tt in range(NT):
                            eng.wait_ge(*jobs.empty("CK", l, tt))
                            eng.wait_ge(*jobs.empty("CQ", l, tt))
                        eng.wait_ge(*jobs.empty("CK", l, NT))
                        if t == 0:
                            last = eng.matmul(bk[:, 0:P], c["qT"][:, h, NLAT:NTOK], c["kT"][:, h, 640:768],
                                              start=True, stop=True)
                        else:
                            cb = t - 1
                            q = c["qT"][:, h, cb * P:(cb + 1) * P]
                            kk = c["kT"][:, h, P:640].rearrange("p (r c) -> p r c", r=ROWS)[:, :, KS[cb]:KS[cb] + 32]
                            eng.matmul(bk[:, 0:P], q, c["kT"][:, h, 0:P], start=True, stop=True)
                            last = eng.matmul(bk[:, P:P + 256], q, kk, start=True, stop=True)
                    last.then_inc(*jobs.filled())

                def turned(u):
                    bk = jobs.open("T", l, u)
                    eng.wait_ge(*jobs.room())
                    eng.wait_ge(*ev.at("prob", l, u))
                    for j in range(n_keys(U[u])):
                        last = eng.transpose(bk[:, j * P:(j + 1) * P], c["p"][:, u % 3, j * P:(j + 1) * P], ident)
                    last.then_inc(*jobs.filled())

                def values(u):
                    kind, t, h = U[u]
                    bk = jobs.open("O", l, u)
                    eng.wait_ge(*jobs.room())
                    eng.wait_ge(*jobs.empty("T", l, u))
                    if kind == "B":
                        kv = h // (HB // KVB)
                        vz = lambda tt: zv[:, tt, C_VB + kv * HD:C_VB + (kv + 1) * HD]
                        if t == 0:
                            vs = [vz(0)]
                        else:
                            lo, nl = b_keys(t)
                            vs = [c["bv"][:, kv * HD:(kv + 1) * HD]] + [vz(1 + lo + i) for i in range(nl)]
                    else:
                        hc = slice(h * HD, (h + 1) * HD)
                        if t == 0:
                            vs = [zv[:, 0, C_VC + h * HD:C_VC + (h + 1) * HD]]
                        else:
                            eng.wait_ge(*ev.at("vp", l))
                            vs = [c["cv"][:, hc]] + [b["vp"][:, t - 1, j, hc] for j in range(2)]
                    for j, v in enumerate(vs):
                        last = eng.matmul(bk[:, 0:HD], c["pT"][:, u % 2, j * P:(j + 1) * P], v,
                                          start=(j == 0), stop=(j == len(vs) - 1))
                    last.then_inc(*jobs.filled())

                for i in range(len(U) + 3):
                    if i < len(U):
                        scores(i)
                    if 0 <= i - 2 < len(U):
                        turned(i - 2)
                    if i >= 3:
                        values(i - 3)
                    if i % 3 == 2 and i >= FILL2:
                        fill(fill2, 1)
                fill(fill2, 99)
                if l + 1 < DEPTH:
                    ada_cols()

                eng.wait_ge(*ev.at("A_out", l))
                for u in range(len(U)):
                    eng.wait_ge(*jobs.empty("O", l, u))
                for k in range(KD):
                    bk = jobs.open("X", l, k)
                    eng.wait_ge(*jobs.room())
                    for t in range(1, NT):
                        last = eng.transpose(bk[:, (t - 1) * P:t * P], mix_cols(t, k), ident)
                    last.then_inc(*jobs.filled())
                for j in range(2):
                    bk = jobs.open("Xp", l, j)
                    eng.wait_ge(*jobs.room())
                    for k in range(4):
                        last = eng.transpose(bk[:, k * P:(k + 1) * P], mix_cols(0, 4 * j + k), ident)
                    last.then_inc(*jobs.filled())
                for k in range(KD):
                    eng.wait_ge(*jobs.empty("X", l, k))
                for j in range(2):
                    eng.wait_ge(*jobs.empty("Xp", l, j))
                w = [unit_view((l, "out", u)) for u in range(N_OUT)]
                for t in range(NT):
                    for half in range(2):
                        bk = jobs.open("Y", l, t, half)
                        eng.wait_ge(*jobs.room())
                        for i in range(2):
                            for k in range(KD):
                                last = eng.matmul(bk[:, i * UN:(i + 1) * UN], hTv[:, k, t * P:(t + 1) * P],
                                                  w[2 * half + i][:, k, :], start=(k == 0), stop=(k == KD - 1))
                        last.then_inc(*jobs.filled())
                        for i in range(2):
                            ev.table[("unit_used", l, "out", 2 * half + i)] = ev.table[("full", jobs.n - 1)]
                for t in range(NT):
                    for j in range(2):
                        bk = jobs.open("RT", l, t, j)
                        eng.wait_ge(*jobs.room())
                        eng.wait_ge(*ev.at("h2", l, t))
                        for k in range(4):
                            last = eng.transpose(bk[:, k * P:(k + 1) * P],
                                                 m["hs"][:, t % 2, (4 * j + k) * P:(4 * j + k + 1) * P], ident)
                        last.then_inc(*jobs.filled())
                    bk = jobs.open("RL", l, t)
                    eng.wait_ge(*jobs.room())
                    eng.wait_ge(*jobs.empty("RT", l, t, 0))
                    eng.wait_ge(*jobs.empty("RT", l, t, 1))
                    eng.wait_ge(*ev.at("ld_wr", l))
                    for k in range(KD):
                        last = eng.matmul(bk[:, 0:36], m["h2T"][:, k, :], wr[:, k, :], start=(k == 0), stop=(k == KD - 1))
                    last.then_inc(*jobs.filled())
                bk = jobs.open("RK", l)
                eng.wait_ge(*jobs.room())
                eng.wait_ge(*ev.at("assign", l))
                for t in range(NT + 1):
                    for s in range(min(t, NT - 1) + 1):
                        w_ = K["strict"] if s == t else K["ones"]
                        last = eng.matmul(bk[:, t * NE:(t + 1) * NE], w_, r["ma"][:, s, :], start=(s == 0),
                                          stop=(s == min(t, NT - 1)))
                last.then_inc(*jobs.filled())
                bk = jobs.open("RX", l)
                eng.wait_ge(*jobs.room())
                eng.wait_ge(*ev.at("listf", l))
                last = eng.transpose(bk[:, 0:NLIST], r["lf"][:, :], ident[0:NLIST, 0:NLIST])
                last.then_inc(*jobs.filled())

                W = MOE[l]
                for n in range(jobs.n - BANKS, jobs.n):
                    eng.wait_ge(*ev.at("free", n))

                def block_x(b_, j, i):
                    eng.wait_ge(W[f"gath{j}"], now(i * 16 + 16))
                    if above_zero(b_):
                        eng.wait_ge(W["xT_act"], now(b_))
                    if above_zero(b_):
                        eng.wait_ge(W["xT_dve"], now(b_))
                    for k in range(KD):
                        last = eng.transpose(bank[k // 4][:, (k % 4) * P:(k % 4 + 1) * P],
                                             e["xg"][:, j, k * P:(k + 1) * P], ident)
                    last.then_inc(W["xT_psum"], 1)

                def block_gu(b_, j, i):
                    eng.wait_ge(W["xT_act"], now(b_ + 1))
                    eng.wait_ge(W["xT_dve"], now(b_ + 1))
                    eng.wait_ge(W[f"w{3 * j}"], now(i * 16 + 16))
                    eng.wait_ge(W[f"w{3 * j + 1}"], now(i * 16 + 16))
                    if above_zero(b_ - 1):
                        eng.wait_ge(W["hm"], now(b_ - 1))
                    wv = ring[:, 3 * j:3 * j + 2, :].rearrange("p u (k n) -> p u k n", k=KD)
                    for k in range(KD):
                        last = eng.matmul(bank[2 + j][:, :], e["xT"][:, j, k * P:(k + 1) * P], wv[:, :, k, :],
                                          start=(k == 0), stop=(k == KD - 1))
                    last.then_inc(W["gu"], 1)

                def block_down(b_, j, i):
                    eng.wait_ge(W["hT"], now(b_ + 1))
                    eng.wait_ge(W[f"w{3 * j + 2}"], now(i * 16 + 16))
                    if above_zero(b_):
                        eng.wait_ge(W["out_act"], now(b_))
                    if above_zero(b_):
                        eng.wait_ge(W["out_dve"], now(b_))
                    wv = ring[:, 3 * j + 2, :].rearrange("p (k n) -> p k n", k=2)
                    for half in range(2):
                        for k in range(2):
                            last = eng.matmul(bank[5 + half][:, :], e["hmT"][:, j, k * P:(k + 1) * P],
                                              wv[:, k, half * 512:(half + 1) * 512], start=(k == 0), stop=(k == 1))
                    last.then_inc(W["out_psum"], 1)

                def block_hT(b_, j):
                    eng.wait_ge(W["hm"], now(b_ + 1))
                    if above_zero(b_):
                        eng.wait_ge(W["hT"], now(b_))
                    for k in range(2):
                        last = eng.transpose(bank[4][:, k * P:(k + 1) * P], e["hm"][:, j, k * P:(k + 1) * P], ident)
                    last.then_inc(W["hT_psum"], 1)

                def turn(i):
                    block_x(i * 2 + 1, 1, i)
                    block_gu(i * 2, 0, i)
                    if not isinstance(i, int) or i > 0:
                        block_down(i * 2 - 1, 1, i - 1)
                    block_hT(i * 2, 0)
                    block_x(i * 2 + 2, 0, i + 1)
                    block_gu(i * 2 + 1, 1, i)
                    block_down(i * 2, 0, i)
                    block_hT(i * 2 + 1, 1)

                block_x(0, 0, 0)
                n = turns(eng, l, turn)
                block_down(n * 2 - 1, 1, n - 1)
                eng.wait_ge(W["out_act"], now(n * 2))
                eng.wait_ge(W["out_dve"], now(n * 2))
                eng.wait_ge(W["xT_act"], now(n * 2 + 1))
                eng.wait_ge(W["xT_dve"], now(n * 2 + 1))

        @block.scalar
        def _(eng):
            act = Engine(ev, "act")

            def bias_rows(l, n):
                if n == 0:
                    for p in range(3):
                        rpb = A["rpb_pad"][l]
                        src = bass.AP(rpb.tensor, rpb.offset + 16 + OFFS[p], [[1, 16], [63, HC * 15], [1, 32]])
                        eng.dma_start(shift_dram[l][p].rearrange("o h r c -> o (h r) c"), src).then_inc(
                            *act.event("shift", l, p, by=16, sem=f"shift{l}"))
                    return
                for q in range(3 * (n - 2), 3 * (n - 1)):
                    if 0 <= q < 3 * ROWS:
                        p, rr = divmod(q, ROWS)
                        if q == 0:
                            eng.wait_ge(*ev.at("shift", l, 2))
                        src = shift_dram[l][p, :, :, 7 - rr:15 - rr, :].rearrange("c h r k -> c h (r k)")
                        eng.dma_start(bias_dram[l][p, rr * 16:(rr + 1) * 16], src).then_inc(
                            *act.event("bias_full", l, p, rr, by=16, sem=f"bias_full{l}"))

            eng.wait_ge(*ev.at("ld_c"))
            eng.activation(cs[:, 1, :, :], cs[:, 0, :, :], ACT.Sigmoid).then_inc(*act.event("sig_c"))

            def ada_copy(todo, n):
                for _ in range(min(n, len(todo))):
                    l, u = todo.pop(0)
                    eng.wait_ge(*ev.at("unit_used", l, "ada", u))
                    if copied:
                        eng.wait_ge(*ev.at("acol", *copied[-1]))
                    eng.activation(arow[:, :], ada_ps[:, P:P + UN], ACT.Copy).then_inc(*act.event("arow", l, u))
                    copied.append((l, u))

            copied = []
            for l in range(DEPTH):
                eng.wait_ge(*ev.at("list_far", l))
            ada_copy([(0, u) for u in range(ADA0)], ADA0)
            for l in range(DEPTH):
                fill1 = [(l, u) for u in range(ADA0, N_ADA)]
                fill2 = [(l + 1, u) for u in range(ADA0)] if l + 1 < DEPTH else []
                eng.wait_ge(*ev.at("modT", l, 0))
                for k in range(0, KD, 2):
                    bk = jobs.bank("H", l, k)
                    eng.wait_ge(*jobs.full("H", l, k))
                    eng.activation(hTv[:, k, P:NTOK], bk[:, :], ACT.Identity,
                                   bias=modT[:, 1, k:k + 1], scale=modT[:, 1, 8 + k:9 + k]).then_inc(*jobs.freed("H", l, k))
                bk = jobs.bank("Hp", l, 0)
                eng.wait_ge(*jobs.full("Hp", l, 0))
                for k in range(4):
                    last = eng.activation(hTv[:, k, 0:P], bk[:, k * P:(k + 1) * P], ACT.Identity,
                                          bias=modT[:, 0, k:k + 1], scale=modT[:, 0, 8 + k:9 + k])
                last.then_inc(*jobs.freed("Hp", l, 0))
                for n in range(N_IN):
                    bias_rows(l, n)
                    for g in range(3):
                        if (3 * n + g) % 2 == 0:
                            bk = jobs.bank("Z", l, n, g)
                            eng.wait_ge(*jobs.full("Z", l, n, g))
                            cnt, nw, out = z_out(n, g)
                            src = bk[:, 0:cnt * UN].rearrange("p (t n) -> p t n", t=cnt)[:, :, 0:nw]
                            eng.activation(out, src, ACT.Copy).then_inc(*jobs.freed("Z", l, n, g))
                g2 = region(small, 160, P, NT, 8)
                eng.wait_ge(*ev.at("g_na", l))
                eng.activation(g2, g2, ACT.Exp).then_inc(*act.step())
                eng.wait_ge(*act.last())
                eng.activation(g2, g2, ACT.Ln, bias=1.0).then_inc(*act.event("g_ln", l))
                for t in range(NT):
                    bk = jobs.bank("AG", l, t)
                    eng.wait_ge(*jobs.full("AG", l, t))
                    eng.activation(a["brow"][:, t * P:(t + 1) * P], bk[0:36, P:2 * P], ACT.Copy).then_inc(*act.event("brow", l, t))
                for t in range(NT):
                    bk = jobs.bank("AQ", l, t)
                    eng.wait_ge(*jobs.full("AQ", l, t))
                    eng.activation(qkA[:, 0, :, t * P:(t + 1) * P],
                                   bk[0:DA, :].rearrange("p (h n) -> p h n", h=HA), ACT.Copy).then_inc(*jobs.freed("AQ", l, t))
                for d in range(2):
                    bk = jobs.bank("AS", l, d)
                    eng.wait_ge(*jobs.full("AS", l, d))
                    eng.activation(a["CT"][:, d, :, :],
                                   bk[0:DA, 0:HA * W97].rearrange("p (h n) -> p h n", h=HA), ACT.Copy).then_inc(*jobs.freed("AS", l, d))
                ada_copy(fill1, 2)
                eng.wait_ge(*ev.at("mo", l))
                eng.activation(a["emo"], a["emo"], ACT.Exp, scale=-1.0).then_inc(*act.event("emo", l))
                for t in range(NT):
                    last = eng.activation(a["scin"][:, t * P:(t + 1) * P], a["gmax"][:, t * P:(t + 1) * P], ACT.Exp,
                                          bias=mp[:, t:t + 1], scale=-1.0)
                last.then_inc(*act.event("scin", l))
                eng.wait_ge(*jobs.empty("AC", l))
                for si, pair in enumerate(STEPS):
                    for d, t in pair:
                        eng.wait_ge(*ev.at("wpre", l, d, t))
                        for h in range(HA):
                            last = eng.activation(a["wt"][:, d, h, :], a["wt"][:, d, h, :], ACT.Exp,
                                                  bias=a["gc"][:, t, 32 * d + h:32 * d + h + 1])
                        last.then_inc(*act.event("w", l, d, t))
                    ada_copy(fill1, 3)
                    if si == 0:
                        for d in range(2):
                            bk = jobs.bank("AU", l, d, 0)
                            eng.wait_ge(*jobs.full("AU", l, d, 0))
                            if d == 0:
                                for dd in range(2):
                                    eng.wait_ge(*ev.at("full", jobs.number(("AS", l, dd))))
                            eng.activation(a["si"][:, d * HA:(d + 1) * HA, :],
                                           bk[0:W97, 0:HA * DA].rearrange("p (h n) -> p h n", h=HA),
                                           ACT.Copy).then_inc(*jobs.freed("AU", l, d, 0))
                eng.wait_ge(*ev.at("hcent", l))
                eng.activation(sq, zv[:, :, 0:D_A], ACT.Square).then_inc(*act.event("hsq", l))
                eng.activation(zv[:, :, C_OA:C_OA + D_A], zv[:, :, C_OA:C_OA + D_A], ACT.Sigmoid).then_inc(*act.event("osig", l))
                bk = jobs.bank("MR", l)
                eng.wait_ge(*jobs.full("MR", l))
                if l > 0:
                    eng.wait_ge(*ev.at("st_modr", l - 1))
                eng.activation(modr.rearrange("p g n -> p (g n)"), bk[0:32, 0:2 * P], ACT.Copy).then_inc(*jobs.freed("MR", l))

                for j, tiles in enumerate(((1, 2), (3, 4), (0, None))):
                    bk = jobs.bank("BK", l, j)
                    eng.wait_ge(*jobs.full("BK", l, j))
                    eng.wait_ge(*ev.at("A_done", l))
                    for i, t in enumerate(tiles):
                        at = 0 if t is None else 640 if t == 0 else t * P
                        last = eng.activation(b["kT"][:, :, at:at + P],
                                              bk[0:HD, 2 * i * P:(2 * i + 2) * P].rearrange("p (v n) -> p v n", v=KVB),
                                              ACT.Copy)
                    last.then_inc(*jobs.freed("BK", l, j))
                U = attention_units()
                for i in range(len(U) + 2):
                    if i < len(U):
                        kind, t, h = U[i]
                        if kind == "B" and h == 0:
                            bk = jobs.bank("BQ", l, t, 1)
                            eng.wait_ge(*jobs.full("BQ", l, t, 1))
                            eng.activation(b["qT"][:, t % 2, 4:6, :],
                                           bk[0:HD, 0:2 * P].rearrange("p (h n) -> p h n", h=2), ACT.Copy,
                                           scale=HD ** -0.5).then_inc(*jobs.freed("BQ", l, t, 1))
                        if kind == "C" and (t, h) == (0, 0):
                            for tt in range(NT + 1):
                                bk = jobs.bank("CK", l, tt)
                                eng.wait_ge(*jobs.full("CK", l, tt))
                                at = 0 if tt == NT else 640 if tt == 0 else tt * P
                                eng.activation(c["kT"][:, :, at:at + P],
                                               bk[0:HD, :].rearrange("p (h n) -> p h n", h=HC), ACT.Copy).then_inc(*jobs.freed("CK", l, tt))
                        nk = n_keys(U[i]) * P
                        bk = jobs.bank("S", l, i)
                        eng.wait_ge(*jobs.full("S", l, i))
                        eng.wait_ge(*ev.at("negmax", l, i))
                        eng.activation(c["p"][:, i % 3, 0:nk], bk[:, 0:nk], ACT.Exp,
                                       bias=sm[:, 0, i:i + 1], accum_out=sm[:, 1, i:i + 1]).then_inc(*jobs.freed("S", l, i))
                        ev.table[("prob", l, i)] = ev.table[("free", jobs.number(("S", l, i)))]
                        if kind == "B":
                            eng.activation(sm[:, 2, i:i + 1], sm[:, 0, i:i + 1], ACT.Exp,
                                           bias=sinkt[:, 0, h:h + 1]).then_inc(*act.event("esink", l, i))
                    if i >= 2:
                        u = i - 2
                        nk = n_keys(U[u]) * P
                        bk = jobs.bank("T", l, u)
                        eng.wait_ge(*jobs.full("T", l, u))
                        eng.activation(c["pT"][:, u % 2, 0:nk], bk[:, 0:nk], ACT.Copy).then_inc(*jobs.freed("T", l, u))
                    if i % 3 == 2 and i >= FILL2:
                        if i == FILL2:
                            eng.wait_ge(*ev.at("st_modr", l))
                        ada_copy(fill2, 1)
                ada_copy(fill2, 99)
                for k in range(0, KD, 2):
                    bk = jobs.bank("X", l, k)
                    eng.wait_ge(*jobs.full("X", l, k))
                    out, src = x_mix_out(k, bk)
                    eng.activation(out, src, ACT.Copy).then_inc(*jobs.freed("X", l, k))
                bk = jobs.bank("Xp", l, 0)
                eng.wait_ge(*jobs.full("Xp", l, 0))
                eng.activation(hTv[:, 0:4, 0:P], bk[:, :].rearrange("p (k n) -> p k n", k=4), ACT.Copy).then_inc(*jobs.freed("Xp", l, 0))

                def ln_hat(w, t):
                    eng.wait_ge(*ev.at("lnnm", w, l, t))
                    eng.activation(x[:, t, :], x[:, t, :], ACT.Identity, bias=lnv[:, t, 4:5],
                                   scale=lnv[:, t, 3:4]).then_inc(*act.event("lnhat", w, l, t))

                for s in range(NT + 4):
                    if 0 <= s - 1 < NT:
                        ln_hat(1, s - 1)
                    if 0 <= s - 4:
                        t = s - 4
                        bk = jobs.bank("RT", l, t, 0)
                        eng.wait_ge(*jobs.full("RT", l, t, 0))
                        if t > 0:
                            eng.wait_ge(*jobs.full("RL", l, t - 1))
                        eng.activation(m["h2T"][:, 0:4, :], bk[:, :].rearrange("p (k n) -> p k n", k=4),
                                       ACT.Copy).then_inc(*jobs.freed("RT", l, t, 0))
                        bk = jobs.bank("RL", l, t)
                        eng.wait_ge(*jobs.full("RL", l, t))
                        eng.activation(r["lg"][:, t, :], bk[:, 0:36], ACT.Copy).then_inc(*jobs.freed("RL", l, t))
                eng.wait_ge(*ev.at("r_gd", l))
                eng.activation(r["t1"][:, :, 0:NG], r["t1"][:, :, 0:NG], ACT.Exp).then_inc(*act.event("r_ge", l))
                eng.wait_ge(*ev.at("r_dl", l))
                eng.activation(s5[:, 6, :], s5[:, 6, :], ACT.Exp).then_inc(*act.event("r_ed", l))

                W = MOE[l]

                def evac_x(b_, j):
                    eng.wait_ge(W["xT_psum"], now(b_ + 1))
                    if above_zero(b_ - 1):
                        eng.wait_ge(W["gu"], now(b_ - 1))
                    eng.activation(e["xT"][:, j, 0:512], bank[0][:, :], ACT.Copy).then_inc(W["xT_act"], 1)

                def evac_sig(b_, j):
                    eng.wait_ge(W["gu"], now(b_ + 1))
                    if above_zero(b_ - 1):
                        eng.wait_ge(W["hm"], now(b_ - 1))
                    eng.activation(e["sig"][:, j, :], bank[2 + j][:, 0:DE], ACT.Sigmoid).then_inc(W["sig"], 1)

                def evac_out(b_, j, i):
                    eng.wait_ge(W["out_psum"], now(b_ + 1))
                    if above_zero(i * 16):
                        eng.wait_ge(W[f"scat{j}"], now(i * 16))
                    eng.activation(e["ob"][:, j, 0:512], bank[5][:, :], ACT.Copy).then_inc(W["out_act"], 1)

                def turn(i):
                    evac_x(i * 2 + 1, 1)
                    evac_sig(i * 2, 0)
                    if not isinstance(i, int) or i > 0:
                        evac_out(i * 2 - 1, 1, i - 1)
                    evac_x(i * 2 + 2, 0)
                    evac_sig(i * 2 + 1, 1)
                    evac_out(i * 2, 0, i)

                evac_x(0, 0)
                n = turns(eng, l, turn)
                evac_out(n * 2 - 1, 1, n - 1)
                eng.wait_ge(W["scat0"], now(n * 16))
                eng.wait_ge(W["scat1"], now(n * 16))
                for s in range(NT + 1):
                    if s < NT:
                        if s >= 2:
                            eng.wait_ge(*ev.at("comb", l, s - 2))
                        for k in range(2):
                            rows = slice((k * NT + s) * P, (k * NT + s + 1) * P)
                            eng.dma_start(o12[:, s % 2, k, :], y_dram[l][rows, :]).then_inc(*act.event("ld_o", l, s, k, by=16, sem=f"ld_o{s % 2}"))
                    if s >= 1:
                        ln_hat(2, s - 1)

        @block.vector
        def _(eng):
            dve = Engine(ev, "dve")
            eng.memset(cond[:, :, :], 0.0).then_inc(*dve.step())
            eng.wait_ge(*dve.last())
            eng.wait_ge(*ev.at("sig_c"))
            eng.tensor_tensor(cond[:, :, 0:2], cs[:, 1, :, :], cs[:, 0, :, :], ALU.mult).then_inc(*dve.event("silu_c"))
            eng.wait_ge(*ev.at("ld_const"))
            eng.tensor_copy(identb[:, :], ident)
            eng.tensor_copy(maskb[:, 0, :], K["mneg_f"])
            eng.tensor_copy(maskb[:, 1, :], K["mneg_b"]).then_inc(*dve.event("maskb"))

            def read_mod(l, grp):
                lo, hi = (0, 16) if grp == 0 else (16, 48)
                eng.wait_ge(*ev.at("ld_bada"))
                eng.wait_ge(*ev.at("acol", l, hi // 2 - 1))
                if grp == 0 and l > 0:
                    for k in range(KD):
                        eng.wait_ge(*jobs.empty("H", l - 1, k))
                    eng.wait_ge(*jobs.empty("Hp", l - 1, 0))
                if grp == 1 and l > 0:
                    eng.wait_ge(*ev.at("full", jobs.number(("MR", l - 1))))
                src = ada_ps[:, 2 * lo:2 * hi].rearrange("p (c g) -> p g c", g=2)
                eng.tensor_tensor(modT[:, :, lo:hi], src, bc(bada[:, l, lo:hi], 1, 2), ALU.add).then_inc(*dve.step())
                eng.wait_ge(*dve.last())
                sc = modT[:, :, 8:16] if grp == 0 else modT[:, :, 32:40]
                eng.tensor_scalar(sc, sc, 1.0, None, ALU.add).then_inc(*dve.event("modT", l, grp))

            read_mod(0, 0)
            for l in range(DEPTH):
                eng.wait_ge(*ev.at("modT", l, 0))
                for k in range(1, KD, 2):
                    bk = jobs.bank("H", l, k)
                    eng.wait_ge(*jobs.full("H", l, k))
                    eng.tensor_scalar(hTv[:, k, P:NTOK], bk[:, :], modT[:, 1, 8 + k:9 + k],
                                      modT[:, 1, k:k + 1], ALU.mult, ALU.add).then_inc(*jobs.freed("H", l, k))
                bk = jobs.bank("Hp", l, 1)
                eng.wait_ge(*jobs.full("Hp", l, 1))
                for k in range(4, KD):
                    last = eng.tensor_scalar(hTv[:, k, 0:P], bk[:, (k - 4) * P:(k - 3) * P], modT[:, 0, 8 + k:9 + k],
                                             modT[:, 0, k:k + 1], ALU.mult, ALU.add)
                last.then_inc(*jobs.freed("Hp", l, 1))
                for n in range(N_IN):
                    for g in range(3):
                        if (3 * n + g) % 2 == 1:
                            bk = jobs.bank("Z", l, n, g)
                            eng.wait_ge(*jobs.full("Z", l, n, g))
                            cnt, nw, out = z_out(n, g)
                            src = bk[:, 0:cnt * UN].rearrange("p (t n) -> p t n", t=cnt)[:, :, 0:nw]
                            eng.tensor_copy(out, src).then_inc(*jobs.freed("Z", l, n, g))
                    if n == C_I // UN:
                        for g in range(3):
                            eng.wait_ge(*jobs.empty("Z", l, n, g))
                        eng.wait_ge(*ev.at("ld_gb", l))
                        g1, g2 = region(small, 120, P, NT, 8), region(small, 160, P, NT, 8)
                        if l > 0:
                            for t in range(NT):
                                eng.wait_ge(*ev.at("x2", l - 1, t))
                        eng.memset(att[:, 1940:1940 + 3 * NT * 36], 0.0)
                        eng.memset(a["gmax"], 0.0)
                        eng.memset(mp[:, :], 0.0).then_inc(*dve.event("mp_zero", l))
                        eng.wait_ge(*dve.last())
                        zi = zv[:, :, C_I:C_I + 8].rearrange("p t (d h) -> p t d h", d=2)
                        gv = a["gi"]
                        for d in range(2):
                            eng.tensor_tensor(gv[:, :, 32 * d:32 * d + 4], zi[:, :, d, :],
                                              bc(gb[:, 4 * d:4 * d + 4], 1, NT), ALU.add)
                        eng.tensor_tensor(g1, zv[:, :, C_F:C_F + 8], bc(gb[:, 8:16], 1, NT), ALU.add).then_inc(*dve.step())
                        eng.wait_ge(*dve.last())
                        eng.scalar_tensor_tensor(out=g2, in0=g1, scalar=-1.0, in1=g1, op0=ALU.mult, op1=ALU.min).then_inc(*dve.event("g_na", l))
                eng.wait_ge(*ev.at("g_ln", l))
                eng.scalar_tensor_tensor(out=a["gf"][:, :, 0:4], in0=g1[:, :, 0:4], scalar=0.0, in1=g2[:, :, 0:4],
                                         op0=ALU.min, op1=ALU.subtract)
                eng.scalar_tensor_tensor(out=a["gbk"][:, :, 32:36], in0=g1[:, :, 4:8], scalar=0.0,
                                         in1=g2[:, :, 4:8], op0=ALU.min, op1=ALU.subtract).then_inc(*dve.event("gates", l))
                for t in range(NT):
                    bk = jobs.bank("AG", l, t)
                    eng.wait_ge(*jobs.full("AG", l, t))
                    eng.wait_ge(*ev.at("brow", l, t))
                    last = eng.tensor_tensor(a["grow"][:, t * P:(t + 1) * P], bk[0:36, 0:P],
                                             a["brow"][:, t * P:(t + 1) * P], ALU.subtract)
                    last.then_inc(*jobs.freed("AG", l, t))
                for t in range(NT):
                    eng.wait_ge(*jobs.empty("AG", l, t))
                eng.wait_ge(*ev.at("ld_m0", l))
                def scan(d, t, nxt):
                    rs = slice(32 * d, 32 * d + 4)
                    cols = slice(t * P, (t + 1) * P)
                    view = (lambda x_: x_[rs, cols]) if d == 0 else (lambda x_: x_[rs, cols][:, ::-1])
                    end = (t + 1) * P - 1 if d == 0 else t * P
                    eng.tensor_tensor_scan(view(a["gmax"]), view(a["grow"]), view(a["grow"]),
                                           mp[rs, t:t + 1], ALU.max, ALU.max).then_inc(*dve.step())
                    eng.wait_ge(*dve.last())
                    if nxt is not None:
                        eng.tensor_tensor(mp[rs, nxt:nxt + 1], a["brow"][rs, end:end + 1],
                                          a["gmax"][rs, end:end + 1], ALU.add).then_inc(*dve.event("mp", l, d, nxt))
                        eng.wait_ge(*dve.last())
                for d in range(2):
                    scan(d, 0, 5)
                for s in range(4):
                    scan(0, 1 + s, 2 + s if s < 3 else None)
                    scan(1, 4 - s, 3 - s if s < 3 else None)
                eng.tensor_tensor(a["emo"], a["brow"], a["gmax"], ALU.add).then_inc(*dve.event("mo", l))
                for t in range(NT):
                    bk = jobs.bank("AK", l, t)
                    eng.wait_ge(*jobs.full("AK", l, t))
                    eng.tensor_scalar(qkA[:, 1, :, t * P:(t + 1) * P],
                                      bk[0:DA, :].rearrange("p (h n) -> p h n", h=HA), DA ** -0.5, None,
                                      ALU.mult).then_inc(*jobs.freed("AK", l, t))
                bk = jobs.bank("AC", l)
                eng.wait_ge(*jobs.full("AC", l))
                eng.tensor_copy(a["gc"].rearrange("p t n -> p (t n)"), bk[:, 0:NT * 72]).then_inc(*jobs.freed("AC", l))
                eng.wait_ge(*jobs.empty("AC", l))
                masks = (K["mneg_f"], K["mneg_b"])
                h4 = lambda ap: ap.rearrange("p (h n) -> p h n", h=HA)
                for si, pair in enumerate(STEPS):
                    for d, t in pair:
                        bk = jobs.bank("AB", l, d, t)
                        eng.wait_ge(*jobs.full("AB", l, d, t))
                        if si > 0:
                            pd, pt = STEPS[si - 1][d]
                            eng.wait_ge(*ev.at("full", jobs.number(("AN", l, pd, pt))))
                        last = eng.tensor_tensor(a["wt"][:, d, :, :], bc(masks[d], 1, HA), h4(bk[:, :]), ALU.subtract)
                        last.then_inc(*jobs.freed("AB", l, d, t))
                        ev.table[("wpre", l, d, t)] = ev.table.get(("free", jobs.number(("AB", l, d, t))))
                        bk = jobs.bank("AI", l, d, t)
                        eng.wait_ge(*jobs.full("AI", l, d, t))
                        end = P - 1 if d == 0 else 0
                        if si > 0:
                            eng.wait_ge(*jobs.empty("AQ", l, t))
                            eng.tensor_tensor(a["qts"][:, d, :, :], qkA[:, 0, :, t * P:(t + 1) * P],
                                              h4(bk[0:DA, :]), ALU.mult).then_inc(*dve.event("qts", l, d, t))
                        eng.tensor_copy(scs[:, d, :], h4(bk[0:DA, :])[:, :, end]).then_inc(*jobs.freed("AI", l, d, t))
                    for d, t in pair:
                        end = P - 1 if d == 0 else 0
                        eng.wait_ge(*ev.at("w", l, d, t))
                        eng.wait_ge(*ev.at("v1", l))
                        if si < len(STEPS) - 1:
                            eng.scalar_tensor_tensor(out=a["wkv"][:, d, :, :], in0=a["v1"][:, t, :, :],
                                                     scalar=DA ** -0.5, in1=bc(a["wt"][:, d, :, end], 2, W97),
                                                     op0=ALU.mult, op1=ALU.mult).then_inc(*dve.event("wkv", l, d, t))
                            eng.wait_ge(*dve.last())
                        bk = jobs.bank("AT", l, d, t)
                        eng.wait_ge(*jobs.full("AT", l, d, t))
                        eng.tensor_tensor(a["wt"][:, d, :, :], a["wt"][:, d, :, :], h4(bk[:, :]), ALU.mult).then_inc(*jobs.freed("AT", l, d, t))
                        ev.table[("sw", l, d, t)] = ev.table.get(("free", jobs.number(("AT", l, d, t))))
                    for d, t in pair:
                        bk = jobs.bank("AN", l, d, t)
                        eng.wait_ge(*jobs.full("AN", l, d, t))
                        nv = bk[:, 0:HA * W97].rearrange("p (h n) -> p h n", h=HA)
                        dn = den[:, d, :]
                        eng.scalar_tensor_tensor(out=dn, in0=nv[:, :, DA], scalar=-1.0,
                                                 in1=a["gc"][:, t, 36 + 32 * d:40 + 32 * d],
                                                 op0=ALU.mult, op1=ALU.max).then_inc(*dve.step())
                        eng.wait_ge(*dve.last())
                        eng.tensor_tensor(dn, dn, nv[:, :, DA], ALU.max).then_inc(*dve.step())
                        eng.wait_ge(*dve.last())
                        eng.reciprocal(dn, dn).then_inc(*dve.step())
                        eng.wait_ge(*dve.last())
                        first = (d == 0) if t == 0 else (d == 0) == (t <= 2)
                        hz = h4(zv[:, t, 0:D_A])
                        if first:
                            eng.tensor_tensor(hz, nv[:, :, 0:DA], bc(dn, 2, DA), ALU.mult).then_inc(*jobs.freed("AN", l, d, t))
                        else:
                            tmp = h4(htmp[:, :])
                            eng.tensor_tensor(tmp, nv[:, :, 0:DA], bc(dn, 2, DA), ALU.mult).then_inc(*jobs.freed("AN", l, d, t))
                            eng.wait_ge(*jobs.empty("AN", l, d, t))
                            eng.tensor_tensor(hz, hz, tmp, ALU.add).then_inc(*dve.step())
                            eng.wait_ge(*dve.last())
                        if 0 < si < len(STEPS) - 1:
                            bk = jobs.bank("AU", l, d, t)
                            eng.wait_ge(*jobs.full("AU", l, d, t))
                            eng.wait_ge(*jobs.empty("AI", l, d, t))
                            C = a["CT"][:, d, :, :]
                            eng.tensor_tensor(C, C, bc(scs[:, d, :], 2, W97), ALU.mult).then_inc(*dve.step())
                            eng.wait_ge(*dve.last())
                            last = eng.tensor_tensor(C, C, bk[0:DA, 0:HA * W97].rearrange("p (h n) -> p h n", h=HA),
                                                     ALU.add)
                            last.then_inc(*jobs.freed("AU", l, d, t))
                            ev.table[("CT", l) + STEPS[si + 1][d]] = ev.table.get(("free", jobs.number(("AU", l, d, t))))
                zh = zv[:, :, 0:D_A].rearrange("p t (h n) -> p t h n", h=HA)
                s20 = lambda i: hst[:, i, :].rearrange("p (t h) -> p t h", t=NT)
                eng.tensor_reduce(s20(0), zh, AX, ALU.add).then_inc(*dve.event("A_done", l))
                eng.wait_ge(*dve.last())
                eng.tensor_scalar(hst[:, 0, :], hst[:, 0, :], -1.0 / DA, None, ALU.mult).then_inc(*dve.step())
                eng.wait_ge(*dve.last())
                for t in range(NT):
                    last = eng.tensor_tensor(zh[:, t], zh[:, t], bc(s20(0)[:, t, :], 2, DA), ALU.add)
                last.then_inc(*dve.event("hcent", l))
                eng.wait_ge(*ev.at("hsq", l))
                eng.tensor_reduce(s20(1), sq.rearrange("p t (h n) -> p t h n", h=HA), AX, ALU.add).then_inc(*dve.step())
                eng.wait_ge(*dve.last())
                eng.tensor_scalar(hst[:, 1, :], hst[:, 1, :], 1.0 / DA, EPS, ALU.mult, ALU.add).then_inc(*dve.event("hvar", l))
                eng.wait_ge(*ev.at("hrstd", l))
                for t in range(NT):
                    last = eng.tensor_tensor(zh[:, t], zh[:, t], bc(s20(2)[:, t, :], 2, DA), ALU.mult)
                last.then_inc(*dve.event("hnorm", l))
                read_mod(l, 1)

                eng.wait_ge(*ev.at("ld_sink", l))
                eng.tensor_scalar(sinkt[:, 1, :], sinkt[:, 0, :], -1.0, None, ALU.mult).then_inc(*dve.step())
                eng.wait_ge(*dve.last())
                U = attention_units()
                for i in range(len(U) + 3):
                    if i < len(U):
                        kind, t, h = U[i]
                        if kind == "B" and h == 0:
                            bk = jobs.bank("BQ", l, t, 0)
                            eng.wait_ge(*jobs.full("BQ", l, t, 0))
                            eng.tensor_scalar(b["qT"][:, t % 2, 0:4, :], h4(bk[0:HD, :]), HD ** -0.5, None,
                                              ALU.mult).then_inc(*jobs.freed("BQ", l, t, 0))
                        if kind == "C" and (t, h) == (0, 0):
                            for tt in range(NT):
                                bk = jobs.bank("CQ", l, tt)
                                eng.wait_ge(*jobs.full("CQ", l, tt))
                                if tt == 0:
                                    last = eng.tensor_scalar(c["qT"][:, :, NLAT:NTOK], h4(bk[0:HD, :]), HD ** -0.5,
                                                             None, ALU.mult)
                                else:
                                    for rr in range(2):
                                        dst = c["qT"][:, :, 0:NLAT].rearrange("p h (b r c) -> p h b r c", b=4, r=ROWS)
                                        src = h4(bk[0:HD, :])[:, :, rr * GRID_W:(rr + 1) * GRID_W]
                                        last = eng.tensor_scalar(dst[:, :, :, 2 * (tt - 1) + rr, :],
                                                                 src.rearrange("p h (b c) -> p h b c", b=4)[:, :, :, ::-1],
                                                                 HD ** -0.5, None, ALU.mult)
                                last.then_inc(*jobs.freed("CQ", l, tt))
                        nk = n_keys(U[i]) * P
                        bk = jobs.bank("S", l, i)
                        eng.wait_ge(*jobs.full("S", l, i))
                        if kind == "C" and t > 0:
                            eng.wait_ge(*ev.at("bias", l, i))
                            eng.tensor_tensor(bk[:, P:nk], bk[:, P:nk], c["bt"][:, i % 2, :], ALU.add).then_inc(*dve.event("biased", l, i))
                            eng.wait_ge(*dve.last())
                        eng.tensor_reduce(sm[:, 0, i:i + 1], bk[:, 0:nk], AX, ALU.max).then_inc(*dve.step())
                        eng.wait_ge(*dve.last())
                        if kind == "B":
                            last = eng.tensor_scalar(sm[:, 0, i:i + 1], sm[:, 0, i:i + 1], -1.0, sinkt[:, 1, h:h + 1],
                                                     ALU.mult, ALU.min)
                        else:
                            last = eng.tensor_scalar(sm[:, 0, i:i + 1], sm[:, 0, i:i + 1], -1.0, None, ALU.mult)
                        last.then_inc(*dve.event("negmax", l, i))
                    if i >= 3:
                        u = i - 3
                        kind, t, h = U[u]
                        eng.wait_ge(*ev.at("prob", l, u))
                        if kind == "B":
                            eng.wait_ge(*ev.at("esink", l, u))
                            eng.tensor_tensor(sm[:, 1, u:u + 1], sm[:, 1, u:u + 1], sm[:, 2, u:u + 1], ALU.add).then_inc(*dve.step())
                            eng.wait_ge(*dve.last())
                        eng.reciprocal(sm[:, 2, u:u + 1], sm[:, 1, u:u + 1]).then_inc(*dve.step())
                        eng.wait_ge(*dve.last())
                        bk = jobs.bank("O", l, u)
                        eng.wait_ge(*jobs.full("O", l, u))
                        at = (C_QB if kind == "B" else C_QC) + h * HD
                        eng.tensor_scalar(zv[:, t, at:at + HD], bk[:, 0:HD], sm[:, 2, u:u + 1], None,
                                          ALU.mult).then_inc(*jobs.freed("O", l, u))
                if l + 1 < DEPTH:
                    read_mod(l + 1, 0)
                for k in range(1, KD, 2):
                    bk = jobs.bank("X", l, k)
                    eng.wait_ge(*jobs.full("X", l, k))
                    out, src = x_mix_out(k, bk)
                    eng.tensor_copy(out, src).then_inc(*jobs.freed("X", l, k))
                bk = jobs.bank("Xp", l, 1)
                eng.wait_ge(*jobs.full("Xp", l, 1))
                eng.tensor_copy(hTv[:, 4:8, 0:P], bk[:, :].rearrange("p (k n) -> p k n", k=4)).then_inc(*jobs.freed("Xp", l, 1))

                def ln_stats(w, t):
                    for i in range(2):
                        last = eng.bn_stats(stats[:, i, :], x[:, t, i * 512:(i + 1) * 512])
                    last.then_inc(*dve.step())
                    eng.wait_ge(*dve.last())
                    eng.bn_aggr(lnv[:, t, 0:2], stats[:, :, :].rearrange("p a b -> p (a b)")).then_inc(*dve.step())
                    eng.wait_ge(*dve.last())
                    eng.tensor_scalar(lnv[:, t, 2:3], lnv[:, t, 1:2], EPS, None, ALU.add).then_inc(*dve.event("lnvar", w, l, t))

                def ln_nm(w, t):
                    eng.wait_ge(*ev.at("lnrstd", w, l, t))
                    eng.tensor_scalar(lnv[:, t, 4:5], lnv[:, t, 0:1], lnv[:, t, 3:4], -1.0, ALU.mult,
                                      ALU.mult).then_inc(*dve.event("lnnm", w, l, t))

                def ln_gain(w, t):
                    eng.wait_ge(*ev.at("lnhat", w, l, t))
                    eng.wait_ge(*ev.at("ld_ln", w, l))
                    eng.tensor_tensor(x[:, t, :], x[:, t, :], m["ln"][:, 0, :], ALU.mult).then_inc(*dve.event("lng", w, l, t))

                for s in range(NT + 4):
                    if s < NT:
                        g = min(s, 1)
                        for half in range(2):
                            cols = slice(half * 512, half * 512 + 512)
                            bk = jobs.bank("Y", l, s, half)
                            eng.wait_ge(*jobs.full("Y", l, s, half))
                            eng.wait_ge(*ev.at("ld_ga", l))
                            eng.tensor_tensor(e["tmp"], bk[:, :], m["ga"][:, g, cols], ALU.mult).then_inc(*jobs.freed("Y", l, s, half))
                            eng.wait_ge(*jobs.empty("Y", l, s, half))
                            eng.scalar_tensor_tensor(out=x[:, s, cols], in0=x[:, s, cols], scalar=ALPHA,
                                                     in1=e["tmp"], op0=ALU.mult, op1=ALU.add).then_inc(*dve.step())
                            eng.wait_ge(*dve.last())
                        ln_stats(1, s)
                    if 0 <= s - 1 < NT:
                        ln_nm(1, s - 1)
                    if 0 <= s - 2 < NT:
                        ln_gain(1, s - 2)
                    if 0 <= s - 3 < NT:
                        t = s - 3
                        eng.wait_ge(*ev.at("x1", l, t))
                        eng.wait_ge(*ev.at("ld_scsh", l))
                        if t >= 2:
                            eng.wait_ge(*ev.at("full", jobs.number(("RT", l, t - 2, 1))))
                            eng.wait_ge(*ev.at("st_h2", l, t - 2))
                        eng.tensor_tensor(m["hs"][:, t % 2, :], x[:, t, :], m["scsh"][:, 0, min(t, 1), :],
                                          ALU.mult).then_inc(*dve.event("hsc", l, t))
                    if 0 <= s - 4:
                        t = s - 4
                        bk = jobs.bank("RT", l, t, 1)
                        eng.wait_ge(*jobs.full("RT", l, t, 1))
                        if t > 0:
                            eng.wait_ge(*jobs.full("RL", l, t - 1))
                        eng.tensor_copy(m["h2T"][:, 4:8, :], bk[:, :].rearrange("p (k n) -> p k n", k=4)).then_inc(*jobs.freed("RT", l, t, 1))
                for t in range(NT):
                    eng.wait_ge(*jobs.empty("RL", l, t))
                lg, le = r["lg"][:, :, 0:NG], r["lg"][:, :, NG:36]
                c5 = lambda i: s5[:, i, :]
                t1g, t2g = r["t1"][:, :, 0:NG], r["t2"][:, :, 0:NG]
                row = lambda k: bc(K[k], 1, NT)
                eng.tensor_reduce(c5(0), lg, AX, ALU.max).then_inc(*dve.step())
                eng.wait_ge(*dve.last())
                eng.tensor_tensor(t1g, lg, bc(c5(0), 2, NG), ALU.subtract).then_inc(*dve.event("r_gd", l))
                eng.tensor_tensor(t2g, lg, bc(c5(0), 2, NG), ALU.is_equal).then_inc(*dve.step())
                eng.wait_ge(*dve.last())
                eng.tensor_tensor(t2g, t2g, row("io4"), ALU.mult).then_inc(*dve.step())
                eng.wait_ge(*dve.last())
                eng.tensor_reduce(c5(1), t2g, AX, ALU.max).then_inc(*dve.step())
                eng.wait_ge(*dve.last())
                eng.tensor_tensor(t2g, t2g, bc(c5(1), 2, NG), ALU.is_equal).then_inc(*dve.step())
                eng.wait_ge(*dve.last())
                eng.tensor_scalar(t2g, t2g, -1.0, -NEG, ALU.add, ALU.mult).then_inc(*dve.step())
                eng.wait_ge(*dve.last())
                g8 = lambda ap: ap.rearrange("p t (g e) -> p t g e", g=NG)
                eng.tensor_tensor(g8(r["lem"]), g8(le), bc(t2g, 3, EPG), ALU.add).then_inc(*dve.step())
                eng.wait_ge(*dve.last())
                eng.wait_ge(*ev.at("r_ge", l))
                eng.tensor_reduce(c5(2), t1g, AX, ALU.add).then_inc(*dve.step())
                eng.wait_ge(*dve.last())
                eng.reciprocal(c5(2), c5(2)).then_inc(*dve.step())
                eng.wait_ge(*dve.last())

                def top(val, hot):
                    eng.tensor_reduce(val, r["lem"], AX, ALU.max).then_inc(*dve.step())
                    eng.wait_ge(*dve.last())
                    eng.tensor_tensor(r["t1"], r["lem"], bc(val, 2, NE), ALU.is_equal).then_inc(*dve.step())
                    eng.wait_ge(*dve.last())
                    eng.tensor_tensor(r["t1"], r["t1"], row("io32"), ALU.mult).then_inc(*dve.step())
                    eng.wait_ge(*dve.last())
                    eng.tensor_reduce(c5(5), r["t1"], AX, ALU.max).then_inc(*dve.step())
                    eng.wait_ge(*dve.last())
                    eng.tensor_tensor(hot, r["t1"], bc(c5(5), 2, NE), ALU.is_equal).then_inc(*dve.step())
                    eng.wait_ge(*dve.last())

                top(c5(3), r["e1"])
                flat = lambda ap: ap.rearrange("p t n -> p (t n)")
                eng.scalar_tensor_tensor(out=flat(r["lem"]), in0=flat(r["e1"]), scalar=2 * NEG,
                                         in1=flat(r["lem"]), op0=ALU.mult, op1=ALU.add).then_inc(*dve.step())
                eng.wait_ge(*dve.last())
                top(c5(4), r["e2"])
                eng.tensor_tensor(c5(6), c5(4), c5(3), ALU.subtract).then_inc(*dve.event("r_dl", l))
                eng.tensor_tensor(r["ma"], r["e1"], r["e2"], ALU.add).then_inc(*dve.event("assign", l))
                eng.wait_ge(*ev.at("r_ed", l))
                eng.tensor_scalar(c5(7), c5(6), 1.0, None, ALU.add).then_inc(*dve.step())
                eng.wait_ge(*dve.last())
                eng.reciprocal(c5(7), c5(7)).then_inc(*dve.step())
                eng.wait_ge(*dve.last())
                eng.tensor_tensor(w12[:, 0, :], c5(7), c5(2), ALU.mult).then_inc(*dve.step())
                eng.wait_ge(*dve.last())
                eng.tensor_tensor(w12[:, 1, :], w12[:, 0, :], c5(6), ALU.mult).then_inc(*dve.step())
                eng.wait_ge(*dve.last())
                bk = jobs.bank("RK", l)
                eng.wait_ge(*jobs.full("RK", l))
                eng.tensor_copy(r["rk"].rearrange("p a b -> p (a b)"), bk[:, 0:6 * NE]).then_inc(*jobs.freed("RK", l))
                eng.wait_ge(*jobs.empty("RK", l))
                cnt = r["rk"][:, NT, :]
                ov, inc, start = r["t2"][:, 0, :], r["t2"][:, 1, :], r["t2"][:, 2, :]
                eng.tensor_scalar(ov, cnt, float(P), None, ALU.is_gt).then_inc(*dve.step())
                eng.wait_ge(*dve.last())
                for j in range(2, NT):
                    eng.scalar_tensor_tensor(out=ov, in0=cnt, scalar=float(j * P), in1=ov, op0=ALU.is_gt,
                                             op1=ALU.add).then_inc(*dve.step())
                    eng.wait_ge(*dve.last())
                eng.tensor_tensor_scan(inc, K["ones"][:, 0:NE], ov, 0.0, ALU.mult, ALU.add).then_inc(*dve.step())
                eng.wait_ge(*dve.last())
                eng.tensor_tensor(start, inc, ov, ALU.subtract).then_inc(*dve.step())
                eng.wait_ge(*dve.last())
                for k, hot in enumerate((r["e1"], r["e2"])):
                    rk, ex, st, far = (c5(8 + 4 * k + q) for q in range(4))
                    for dst, by in ((rk, r["rk"][:, 0:NT, :]), (ex, row("eid")), (st, bc(start, 1, NT))):
                        eng.tensor_tensor(r["t1"], hot, by, ALU.mult).then_inc(*dve.step())
                        eng.wait_ge(*dve.last())
                        eng.tensor_reduce(dst, r["t1"], AX, ALU.add).then_inc(*dve.step())
                        eng.wait_ge(*dve.last())
                    eng.tensor_scalar(far, rk, float(P), None, ALU.is_ge).then_inc(*dve.step())
                    eng.wait_ge(*dve.last())
                    eng.tensor_tensor(st, st, ex, ALU.subtract).then_inc(*dve.step())
                    eng.wait_ge(*dve.last())
                    eng.tensor_scalar(st, st, float(P), float((NE - 1) * P), ALU.mult, ALU.add).then_inc(*dve.step())
                    eng.wait_ge(*dve.last())
                    eng.tensor_tensor(st, st, far, ALU.mult).then_inc(*dve.step())
                    eng.wait_ge(*dve.last())
                    eng.scalar_tensor_tensor(out=rk, in0=ex, scalar=float(P), in1=rk, op0=ALU.mult,
                                             op1=ALU.add).then_inc(*dve.step())
                    eng.wait_ge(*dve.last())
                    eng.tensor_tensor(rk, rk, st, ALU.add).then_inc(*dve.step())
                    eng.wait_ge(*dve.last())
                    last = eng.tensor_copy(posi[:, k * NT:(k + 1) * NT], rk)
                last.then_inc(*dve.event("slots", l))
                o1 = r["ov"][0:1, :, :]
                eng.tensor_tensor(o1, bc(r["t2"][0:1, 1, :], 1, 10), bc(K["io10"][0:1, :], 2, NE), ALU.is_le).then_inc(*dve.step())
                eng.wait_ge(*dve.last())
                eng.tensor_reduce(ctlf[:, 2:12], o1, AX, ALU.add).then_inc(*dve.step())
                eng.wait_ge(*dve.last())
                eng.tensor_scalar(ctlf[:, 2:12], ctlf[:, 2:12], float(NE - 1), None, ALU.min).then_inc(*dve.step())
                eng.wait_ge(*dve.last())
                eng.memset(ctlf[:, 0:1], float(NE - 2))
                eng.memset(ctlf[:, 1:2], float(NE - 1))
                eng.memset(ctlf[:, 12:13], float(NE // 2 - 2)).then_inc(*dve.step())
                eng.wait_ge(*dve.last())
                for j in range(0, 2 * NT, 2):
                    eng.scalar_tensor_tensor(out=ctlf[:, 12:13], in0=r["t2"][0:1, 1, NE - 1:NE],
                                             scalar=float(j), in1=ctlf[:, 12:13], op0=ALU.is_gt, op1=ALU.add).then_inc(*dve.step())
                    eng.wait_ge(*dve.last())
                eng.tensor_scalar(ctlf[:, 13:14], ctlf[:, 12:13], float(3 - NE // 2), None, ALU.add).then_inc(*dve.step())
                eng.wait_ge(*dve.last())
                eng.memset(ctlf[:, 14:15], 0.0).then_inc(*dve.step())
                eng.wait_ge(*dve.last())
                eng.tensor_copy(ctl[0:1, 0:15], ctlf[:, 0:15]).then_inc(*dve.event("ctl", l))
                eng.wait_ge(*ev.at("list_back", l))
                eng.tensor_copy(r["lf"], listi).then_inc(*dve.event("listf", l))
                bk = jobs.bank("RX", l)
                eng.wait_ge(*jobs.full("RX", l))
                lx = r["t1"].rearrange("p t n -> p (t n)")[:, 0:NLIST]
                lfar = r["lem"].rearrange("p t n -> p (t n)")[:, 0:NLIST]
                eng.tensor_copy(lx, bk[:, 0:NLIST]).then_inc(*dve.step())
                eng.wait_ge(*dve.last())
                eng.tensor_scalar(lfar, lx, float(NTOK), float(-NTOK), ALU.is_ge, ALU.mult).then_inc(*dve.step())
                eng.wait_ge(*dve.last())
                eng.tensor_copy(sidx[:, :], lx)
                eng.tensor_tensor(gidx[:, :], lx, lfar, ALU.add).then_inc(*jobs.freed("RX", l))
                ev.table[("lists", l)] = ev.table.get(("free", jobs.number(("RX", l))))

                W = MOE[l]

                def evac_x(b_, j):
                    eng.wait_ge(W["xT_psum"], now(b_ + 1))
                    if above_zero(b_ - 1):
                        eng.wait_ge(W["gu"], now(b_ - 1))
                    eng.tensor_copy(e["xT"][:, j, 512:1024], bank[1][:, :]).then_inc(W["xT_dve"], 1)

                def hidden(b_, j):
                    eng.wait_ge(W["sig"], now(b_ + 1))
                    eng.tensor_tensor(e["sig"][:, j, :], e["sig"][:, j, :], bank[2 + j][:, 0:DE], ALU.mult)\
                        .then_inc(W["hm_part"], 1)
                    eng.wait_ge(W["hm_part"], now(b_ + 1))
                    if above_zero(b_ - 1):
                        eng.wait_ge(W["hT_psum"], now(b_ - 1))
                    eng.tensor_tensor(e["hm"][:, j, :], e["sig"][:, j, :], bank[2 + j][:, DE:2 * DE], ALU.mult)\
                        .then_inc(W["hm"], 1)

                def evac_out(b_, j, i):
                    eng.wait_ge(W["out_psum"], now(b_ + 1))
                    if above_zero(i * 16):
                        eng.wait_ge(W[f"scat{j}"], now(i * 16))
                    eng.tensor_copy(e["ob"][:, j, 512:1024], bank[6][:, :]).then_inc(W["out_dve"], 1)

                def evac_hT(b_, j):
                    eng.wait_ge(W["hT_psum"], now(b_ + 1))
                    if above_zero(b_ - 1):
                        eng.wait_ge(W["out_psum"], now(b_ - 1))
                    eng.tensor_copy(e["hmT"][:, j, :], bank[4][:, 0:2 * P]).then_inc(W["hT"], 1)

                def turn(i):
                    evac_x(i * 2 + 1, 1)
                    hidden(i * 2, 0)
                    if not isinstance(i, int) or i > 0:
                        evac_out(i * 2 - 1, 1, i - 1)
                    evac_hT(i * 2, 0)
                    evac_x(i * 2 + 2, 0)
                    hidden(i * 2 + 1, 1)
                    evac_out(i * 2, 0, i)
                    evac_hT(i * 2 + 1, 1)

                evac_x(0, 0)
                n = turns(eng, l, turn)
                evac_out(n * 2 - 1, 1, n - 1)
                for s in range(NT + 2):
                    if s < NT:
                        g = min(s, 1)
                        for k in range(2):
                            eng.wait_ge(*ev.at("ld_o", l, s, k))
                        o1_, o2_ = o12[:, s % 2, 0, :], o12[:, s % 2, 1, :]
                        eng.tensor_scalar(o1_, o1_, w12[:, 0, s:s + 1], None, ALU.mult).then_inc(*dve.step())
                        eng.wait_ge(*dve.last())
                        eng.scalar_tensor_tensor(out=o1_, in0=o2_, scalar=w12[:, 1, s:s + 1], in1=o1_,
                                                 op0=ALU.mult, op1=ALU.add).then_inc(*dve.step())
                        eng.wait_ge(*dve.last())
                        eng.wait_ge(*ev.at("ld_gf", l))
                        eng.tensor_tensor(o1_, o1_, m["gf"][:, g, :], ALU.mult).then_inc(*dve.step())
                        eng.wait_ge(*dve.last())
                        eng.scalar_tensor_tensor(out=x[:, s, :], in0=x[:, s, :], scalar=ALPHA, in1=o1_,
                                                 op0=ALU.mult, op1=ALU.add).then_inc(*dve.event("comb", l, s))
                        eng.wait_ge(*dve.last())
                        ln_stats(2, s)
                    if 0 <= s - 1 < NT:
                        ln_nm(2, s - 1)
                    if 0 <= s - 2 < NT:
                        ln_gain(2, s - 2)

        @block.gpsimd
        def _(eng):
            pool = Engine(ev, "pool")

            def ld(dst, src, *key, sem=None):
                eng.dma_start(dst, src).then_inc(*pool.event(*key, by=16, sem=sem or str(key[0])))

            eng.iota(ids[:, :], pattern=[[P, 2 * NT]], base=0, channel_multiplier=1)
            eng.memset(flist, FAR).then_inc(*pool.step())
            eng.wait_ge(*pool.last())
            for l in range(DEPTH):
                ld(list_dram[l].rearrange("(b p) o -> b (p o)", p=P), flist, "list_far", l, sem=f"list_far{l}")
            for l in range(DEPTH):
                eng.wait_ge(*ev.at("list_far", l))
            for l in range(DEPTH):
                if l > 0:
                    for t in range(NT):
                        eng.wait_ge(*ev.at("x2", l - 1, t))
                        dve_free = ("full", jobs.number(("RL", l - 1, t)))
                        eng.wait_ge(*ev.at(*dve_free))
                ld(gb[:, 0:8], A["b_a_i"][l].rearrange("d h -> (d h)").partition_broadcast(P), "ld_gb0", l)
                ld(gb[:, 8:16], A["b_a_f"][l].rearrange("d h -> (d h)").partition_broadcast(P), "ld_gb", l, sem="ld_gb0")
                ld(sinkt[:, 0, :], A["b_sink"][l].partition_broadcast(P), "ld_sink", l)
                ld(wr[:, :, :].rearrange("p k n -> p (k n)"), A["w_r"][l], "ld_wr", l)
                ld(a["hn"], A["w_a_hnorm"][l].partition_broadcast(P), "ld_hn", l)
                ld(a["si"][0:DA, :, :], A["state_a_C"][0, l].rearrange("d h v k -> v (d h) k"), "ld_si0", l)
                ld(a["si"][DA:W97, :, :], A["state_a_n"][0, l].rearrange("d h k -> (d h) k").unsqueeze(0), "ld_si", l,
                   sem="ld_si0")
                eng.wait_ge(*ev.at("mp_zero", l))
                ld(mp[0:HA, 1:2], A["state_a_m"][0, l, 0].unsqueeze(1), "ld_m00", l)
                ld(mp[32:32 + HA, 4:5], A["state_a_m"][0, l, 1].unsqueeze(1), "ld_m0", l, sem="ld_m00")
                for n in range((C_VA + D_A + UN - 1) // UN):
                    for g in range(3):
                        eng.wait_ge(*jobs.empty("Z", l, n, g))
                for t in range(NT):
                    eng.tensor_copy(a["v1"][:, t, :, 0:DA], zv[:, t, C_VA:C_VA + D_A].rearrange("p (h n) -> p h n", h=HA))
                v1f = a["v1"].rearrange("p t h n -> p (t h) n")
                eng.memset(v1f[:, :, DA:W97], 1.0).then_inc(*pool.event("v1", l))
                for n in range(-(-C_VB // UN)):
                    for g in range(3):
                        eng.wait_ge(*jobs.empty("Z", l, n, g))
                for t in range(1, NT):
                    cosv = K["cos"][:, (t - 1) * HD:t * HD]
                    sinv = K["sin"][:, (t - 1) * HD:t * HD].rearrange("p (f q n) -> p f q n", f=2, q=2)
                    for hh in range(0, 8, 4):
                        at = C_QB + hh * HD
                        zz = zv[:, t, at:at + 4 * HD]
                        z4 = zz.rearrange("p (h n) -> p h n", h=4)
                        zq = zz.rearrange("p (h f q n) -> p h f q n", h=4, f=2, q=2)
                        ra = a["rope"][:, 0, :]
                        rb = a["rope"][:, 1, :].rearrange("p (h f q n) -> p h f q n", h=4, f=2, q=2)
                        for f in range(2):
                            for q in range(2):
                                pool_last = eng.tensor_tensor(rb[:, :, f, q, :], zq[:, :, f, 1 - q, :],
                                                              bc(sinv[:, f, q, :], 1, 4), ALU.mult)
                        eng.tensor_tensor(ra.rearrange("p (h n) -> p h n", h=4), z4, bc(cosv, 1, 4),
                                          ALU.mult).then_inc(*pool.step())
                        eng.wait_ge(*pool.last())
                        last = eng.tensor_tensor(zz, ra, a["rope"][:, 1, :], ALU.add)
                        last.then_inc(*pool.event("rope_half" if hh == 0 else "rope", l, t))
                        eng.wait_ge(*pool.last())
                for n in range(N_IN):
                    for g in range(3):
                        eng.wait_ge(*jobs.empty("Z", l, n, g))
                for name, col, w_ in (("new_b_k", C_KB, D_KVB), ("new_b_v", C_VB, D_KVB), ("new_c_k", C_KC, D_C),
                                      ("new_c_v", C_VC, D_C)):
                    ld(A[name][0, l].rearrange("s h d -> s (h d)"), zv[:, 0, col:col + w_], "st_cache", l, name)
                for d in range(2):
                    eng.wait_ge(*ev.at("mp", l, d, 5))
                    ld(A["new_m"][0, l, d].unsqueeze(1), mp[32 * d:32 * d + HA, 5:6], "st_state", l, d, "m")
                for d in range(2):
                    eng.wait_ge(*jobs.empty("AU", l, d, 0))
                    sid = a["si"][:, d * HA:(d + 1) * HA, :]
                    ld(A["new_C"][0, l, d].rearrange("h v k -> v h k"), sid[0:DA], "st_state", l, d, "C")
                    ld(A["new_n"][0, l, d].unsqueeze(0), sid[DA:W97], "st_state", l, d, "n")
                eng.wait_ge(*ev.at("hvar", l))
                eng.tensor_tensor(hst[:, 2, :], hst[:, 1, :], K["pm05"].broadcast_to([P, 20]), ALU.pow).then_inc(*pool.event("hrstd", l))
                eng.wait_ge(*ev.at("A_done", l))
                for d in range(2):
                    eng.wait_ge(*ev.at("st_state", l, d, "n"))
                ld(c["bk"], A["cache_b_k"][0, l].rearrange("s h d -> s (h d)"), "ld_cache", l, 0)
                ld(c["bv"], A["cache_b_v"][0, l].rearrange("s h d -> s (h d)"), "ld_cache", l, 1)
                ld(c["ck"], A["cache_c_k"][0, l].rearrange("s h d -> s (h d)"), "ld_cache", l, 2)
                ld(c["cv"], A["cache_c_v"][0, l].rearrange("s h d -> s (h d)"), "ld_cache", l)
                for cb in range(4):
                    for kr in range(ROWS):
                        p0 = (kr % 2) * GRID_W + KS[cb]
                        ld(b["vp"][(kr % 4) * 32:(kr % 4 + 1) * 32, cb, kr // 4, :],
                           zv[p0:p0 + 32, 1 + kr // 2, C_VC:C_VC + D_C],
                           *(("vp", l) if (cb, kr) == (3, ROWS - 1) else ("vp", l, cb, kr)))
                for t in range(NT):
                    eng.wait_ge(*ev.at("hnorm", l))
                    eng.wait_ge(*ev.at("ld_hn", l))
                    last = eng.tensor_tensor(zv[:, t, 0:D_A], zv[:, t, 0:D_A], a["hn"], ALU.mult)
                last.then_inc(*pool.step())
                eng.wait_ge(*pool.last())
                eng.wait_ge(*ev.at("osig", l))
                for t in range(NT):
                    last = eng.tensor_tensor(zv[:, t, 0:D_A], zv[:, t, 0:D_A], zv[:, t, C_OA:C_OA + D_A], ALU.mult)
                last.then_inc(*pool.event("A_out", l))
                eng.wait_ge(*jobs.empty("MR", l))
                ld(mod_dram[l].rearrange("g c n -> c g n"), modr, "st_modr", l)
                U = attention_units()
                latent = [i for i, (kind, t, h) in enumerate(U) if kind == "C" and t > 0]
                eng.wait_ge(*ev.at("bias_full", l, 2, ROWS - 1))
                for i in latent:
                    _, t, h = U[i]
                    if i - 2 in latent:
                        eng.wait_ge(*ev.at("biased", l, i - 2))
                    pt = PAT[t - 1]
                    bt = c["bt"][:, i % 2, :]
                    ld(bt, bias_dram[l][pt, :, h, :], "ld_bt", l, i)
                    eng.wait_ge(*ev.at("ld_bt", l, i))
                    bt8 = bt.rearrange("p (r c) -> p r c", r=ROWS)
                    eng.tensor_tensor(bt8, bt8, bc(K["natmask"][:, pt * 32:(pt + 1) * 32], 1, ROWS), ALU.add).then_inc(*pool.event("bias", l, i))
                eng.wait_ge(*ev.at("full", jobs.number(("Xp", l, 1))))
                eng.wait_ge(*ev.at("st_modr", l))
                mr = mod_dram[l].rearrange("g a b -> (g a b)")

                def mrow(g, q):
                    at = (g * 32 + q * 8) * P
                    return mr[at:at + D].partition_broadcast(P)

                def ld_ln(w):
                    ld(m["ln"][:, 0, :], A["ln_g"][l, w - 1].partition_broadcast(P), "ld_lng", w, l)
                    ld(m["ln"][:, 1, :], A["ln_b"][l, w - 1].partition_broadcast(P), "ld_ln", w, l, sem="ld_lng")

                for g in range(2):
                    ld(m["ga"][:, g, :], mrow(g, 0), *(("ld_ga", l) if g else ("ld_ga", l, 0)))
                ld_ln(1)
                for g in range(2):
                    ld(m["scsh"][:, 1, g, :], mrow(g, 1), "ld_scsh", l, g, "sh")
                    ld(m["scsh"][:, 0, g, :], mrow(g, 2), *(("ld_scsh", l) if g else ("ld_scsh", l, 0)))
                for g in range(2):
                    ld(m["gf"][:, g, :], mrow(g, 3), *(("ld_gf", l) if g else ("ld_gf", l, 0)))

                def ln_rstd(w, t):
                    eng.wait_ge(*ev.at("lnvar", w, l, t))
                    eng.tensor_tensor(lnv[:, t, 3:4], lnv[:, t, 2:3], K["pm05"], ALU.pow).then_inc(*pool.event("lnrstd", w, l, t))

                def ln_shift(w, t):
                    eng.wait_ge(*ev.at("lng", w, l, t))
                    eng.wait_ge(*ev.at("ld_ln", w, l))
                    eng.tensor_tensor(x[:, t, :], x[:, t, :], m["ln"][:, 1, :], ALU.add).then_inc(*pool.event(f"x{w}", l, t))
                    eng.wait_ge(*pool.last())

                for s in range(NT + 3):
                    if s < NT:
                        ln_rstd(1, s)
                    if 0 <= s - 2 < NT:
                        ln_shift(1, s - 2)
                    if 0 <= s - 3 < NT:
                        t = s - 3
                        eng.wait_ge(*ev.at("hsc", l, t))
                        hs = m["hs"][:, t % 2, :]
                        eng.wait_ge(*ev.at("ld_scsh", l))
                        eng.tensor_tensor(hs, hs, m["scsh"][:, 1, min(t, 1), :], ALU.add).then_inc(*pool.event("h2", l, t))
                        eng.wait_ge(*pool.last())
                        ld(h2_dram[l][t * P:(t + 1) * P, :], hs, "st_h2", l, t, sem=f"st_h2_{t % 2}")
                ld_ln(2)
                eng.wait_ge(*ev.at("x1", l, NT - 1))
                eng.memset(e["xg"][:, 0, :], 0.0)
                eng.memset(e["xg"][:, 1, :], 0.0).then_inc(*pool.step())
                eng.wait_ge(*pool.last())
                eng.wait_ge(*ev.at("slots", l))
                for q in range(2 * NT):
                    eng.indirect_dma_start(list_dram[l], bass.IndirectOffsetOnAxis(ap=posi[:, q:q + 1], axis=0),
                                           ids[:, q:q + 1], None).then_inc(*pool.event("list_in", l, q, by=16, sem="list_in"))
                eng.wait_ge(*ev.at("list_in", l, 2 * NT - 1))
                ld(listi, list_dram[l].rearrange("(b p) o -> b (p o)", p=P), "list_back", l)
                for t in range(NT):
                    eng.wait_ge(*ev.at("st_h2", l, t))
                eng.wait_ge(*ev.at("lists", l))
                W = MOE[l]

                nought = [0]

                def last_row(b_, rows):
                    return rows - 1 if isinstance(b_, int) else now(b_) * nought[0] + (rows - 1)

                def gather(b_, j, first):
                    col = gidx[:, b_:b_ + 1] if isinstance(b_, int) else gidx[:, bass.ds(now(b_), 1)]
                    if above_zero(b_ - 1):
                        eng.wait_ge(W["xT_psum"], now(b_ - 1))
                    if not first:
                        if above_zero(pair_count(b_, j)):
                            eng.wait_ge(W[f"gath{j}"], now(pair_count(b_, j)))
                    eng.tensor_copy(cur[:, j:j + 1], col).then_inc(W["cur_gath"], 1)
                    eng.wait_ge(W["cur_gath"], now(b_ + 1))
                    eng.indirect_dma_start(e["xg"][:, j, :], None, h2_dram[l],
                                           bass.IndirectOffsetOnAxis(ap=cur[:, j:j + 1], axis=0),
                                           bounds_check=last_row(b_, NTOK), oob_is_err=False).then_inc(W[f"gath{j}"], 16)

                def pair_count(b_, j):
                    return (b_ - j) * 8

                def scatter(b_, j):
                    col = sidx[:, b_:b_ + 1] if isinstance(b_, int) else sidx[:, bass.ds(now(b_), 1)]
                    eng.wait_ge(W["out_act"], now(b_ + 1))
                    eng.wait_ge(W["out_dve"], now(b_ + 1))
                    if above_zero(pair_count(b_, j)):
                        eng.wait_ge(W[f"scat{j}"], now(pair_count(b_, j)))
                    eng.tensor_copy(cur[:, 2 + j:3 + j], col).then_inc(W["cur_scat"], 1)
                    eng.wait_ge(W["cur_scat"], now(b_ + 1))
                    eng.indirect_dma_start(y_dram[l], bass.IndirectOffsetOnAxis(ap=cur[:, 2 + j:3 + j], axis=0),
                                           e["ob"][:, j, :], None,
                                           bounds_check=last_row(b_, 2 * NTOK), oob_is_err=False).then_inc(W[f"scat{j}"], 16)

                def turn(i):
                    gather(i * 2 + 2, 0, False)
                    if not isinstance(i, int) or i > 0:
                        scatter(i * 2 - 1, 1)
                    gather(i * 2 + 3, 1, False)
                    scatter(i * 2, 0)

                gather(0, 0, True)
                gather(1, 1, True)
                eng.wait_ge(*ev.at("ctl", l))
                nought[0] = eng.value_load(ctl[0:1, 14:15], min_val=0, max_val=1)
                n = turns(eng, l, turn)
                scatter(n * 2 - 1, 1)
                eng.wait_ge(W["gath0"], now((n + 1) * 16))
                eng.wait_ge(W["gath1"], now((n + 1) * 16))
                for s in range(NT + 2):
                    if s < NT:
                        ln_rstd(2, s)
                    if 0 <= s - 2:
                        ln_shift(2, s - 2)
                eng.wait_ge(*ev.at("vp", l))
                eng.wait_ge(*ev.at("st_cache", l, "new_c_v"))
                for d in range(2):
                    eng.wait_ge(*ev.at("st_state", l, d, "n"))


    return ev.table


_OUTS = [("y_prompt", (1, SEQ, D)), ("y_sample", (1, NLAT, D)), ("new_C", (1, DEPTH, 2, HA, DA, DA)),
         ("new_n", (1, DEPTH, 2, HA, DA)), ("new_m", (1, DEPTH, 2, HA)),
         ("new_b_k", (1, DEPTH, SEQ, KVB, HD)), ("new_b_v", (1, DEPTH, SEQ, KVB, HD)),
         ("new_c_k", (1, DEPTH, SEQ, HC, HD)), ("new_c_v", (1, DEPTH, SEQ, HC, HD))]


def kernel(x_prompt, x_sample, state_a_C, state_a_n, state_a_m, cache_b_k, cache_b_v, cache_c_k, cache_c_v,
           c, c_ctx, w_in, b_a_i, b_a_f, w_a_hnorm, b_sink, rpb, w_out, w_ada, b_ada, ln_g, ln_b,
           w_router_grp, w_router_exp, w_e_gate, w_e_up, w_e_down):
    import concourse.bacc as _bacc
    from concourse.bass_utils import run_bass_kernel_spmd as _run

    def units_of(w, n):
        w = np.asarray(w)
        if w.shape[2] < n * UN:
            w = np.concatenate([w, np.zeros((w.shape[0], D, n * UN - w.shape[2]), w.dtype)], 2)
        return w.reshape(DEPTH, KD, P, n, UN).transpose(0, 3, 2, 1, 4).reshape(DEPTH, n, P, KD * UN)

    def expert_cols(w):
        return np.asarray(w).reshape(DEPTH, NE, KD, P, DE).transpose(0, 1, 3, 2, 4).reshape(DEPTH, NE, 1, P, KD * DE)

    down = np.asarray(w_e_down).reshape(DEPTH, NE, 2, P, D).transpose(0, 1, 3, 2, 4).reshape(DEPTH, NE, 1, P, 2 * D)
    w_r = np.concatenate([np.asarray(w_router_grp), np.asarray(w_router_exp)], 2)
    conds = np.stack([np.asarray(c_ctx), np.asarray(c)[0]], 1)
    arrays = {
        "const": constants(),
        "x_all": np.concatenate([np.asarray(x_prompt)[0], np.asarray(x_sample)[0]], 0),
        "c_T": conds.reshape(KD, P, 2).transpose(1, 0, 2).reshape(P, KD * 2),
        "bada_T": np.asarray(b_ada).reshape(DEPTH, 48, P).transpose(2, 0, 1).reshape(P, DEPTH * 48),
        "w_ada": units_of(w_ada, N_ADA), "w_in": units_of(w_in, N_IN), "w_out": units_of(w_out, N_OUT),
        "w_exp": np.concatenate([expert_cols(w_e_gate), expert_cols(w_e_up), down], 2),
        "w_r": w_r.reshape(DEPTH, KD, P, 36).transpose(0, 2, 1, 3).reshape(DEPTH, P, KD * 36),
        "rpb_pad": np.pad(np.asarray(rpb), ((0, 0), (0, 0), (0, 0), (16, 16))),
        "state_a_C": state_a_C, "state_a_n": state_a_n, "state_a_m": state_a_m, "cache_b_k": cache_b_k,
        "cache_b_v": cache_b_v, "cache_c_k": cache_c_k, "cache_c_v": cache_c_v, "b_a_i": b_a_i, "b_a_f": b_a_f,
        "w_a_hnorm": w_a_hnorm, "b_sink": b_sink, "ln_g": ln_g, "ln_b": ln_b,
    }
    arrays = {k: np.ascontiguousarray(v) for k, v in arrays.items()}
    table = {}
    for _ in range(2):
        nc = _bacc.Bacc("TRN2", target_bir_lowering=False, num_devices=1)
        A = {k: nc.dram_tensor(f"in_{k}", v.shape, mybir.dt.from_np(v.dtype), kind="ExternalInput").ap()
             for k, v in arrays.items()}
        for name, shape in _OUTS:
            A[name] = nc.dram_tensor(f"out_{name}", shape, F32, kind="ExternalOutput").ap()
        table = program(nc, A, table)
    r = _run(nc, [{f"in_{k}": v for k, v in arrays.items()}], core_ids=[0])
    return tuple(r.results[0][f"out_{name}"] for name, _ in _OUTS)
```
